# Optimizing a Trainium2 kernel written in Bass

```python
import math
import jax
import jax.numpy as jnp
from jax import lax
import numpy as np

D_MODEL = 1024
BATCH = 1
SEQ = 1024
DEPTH = 1
DEC_BATCH = 8
DEC_SEQ = 16
PAST_LEN = 512

CHUNK = 64
N_META = 16
EPS = 1e-6
POOL_GROUPS = 4
POOL_WINDOWS = (2, 4, 8, 16)
POOL_GROUP_DIM = D_MODEL // POOL_GROUPS
POOL_WIDTH = POOL_GROUPS * POOL_GROUP_DIM
POOL_STATE = max(POOL_WINDOWS) - 1
N_HEADS = 8
N_KV_HEADS = 2
HEAD_DIM = D_MODEL // N_HEADS
KV_REP = N_HEADS // N_KV_HEADS
Q_WIDTH = N_HEADS * HEAD_DIM
KV_WIDTH = N_KV_HEADS * HEAD_DIM
N_IDX_HEADS = 4
IDX_DIM = 64
IDX_TOPK = 256
IDX_W_SCALE = (N_IDX_HEADS * IDX_DIM) ** -0.5
ATTN_SCALE = HEAD_DIM ** -0.5
QUERY_BLOCK = 128
ROPE_THETA = 500000.0
ROT_FRACTION = 4
IN_WIDTHS = (POOL_WIDTH, Q_WIDTH, KV_WIDTH, KV_WIDTH, N_IDX_HEADS * IDX_DIM, IDX_DIM, N_IDX_HEADS, D_MODEL, D_MODEL)
SPLIT_POINTS = tuple(int(s) for s in np.cumsum(IN_WIDTHS)[:-1])
IN_WIDTH = sum(IN_WIDTHS)
N_EXPERT_GROUPS = 4
EXPERTS_PER_GROUP = 8
N_EXPERTS = N_EXPERT_GROUPS * EXPERTS_PER_GROUP
EXPERT_TOPK = 2
D_EXPERT = 128

kernel_name = 'pool_dsa_hiermoe_streaming_step'

def rms_norm(x, g):
    xf = x.astype(jnp.float32)
    y = xf * lax.rsqrt(jnp.mean(xf * xf, axis=-1, keepdims=True) + EPS) * g.astype(jnp.float32)
    return y.astype(x.dtype)

def chunk_index(p):
    return jnp.where(p < N_META, 0, (p - N_META) // CHUNK + 1)

def rope(x, pos):
    d = x.shape[-1]
    rot = d // ROT_FRACTION
    half = rot // 2
    inv = jnp.exp(-math.log(ROPE_THETA) * jnp.arange(half, dtype=jnp.float32) * (2.0 / rot))
    ang = pos.astype(jnp.float32)[:, None] * inv[None, :]
    cos = jnp.cos(ang)[:, None, :]
    sin = jnp.sin(ang)[:, None, :]
    xf = x.astype(jnp.float32)
    x1 = xf[..., :half]
    x2 = xf[..., half:rot]
    return jnp.concatenate([x1 * cos - x2 * sin, x2 * cos + x1 * sin, xf[..., rot:]], axis=-1).astype(x.dtype)

def in_project(h, w_in, pos):
    B, S, _ = h.shape
    z_pool, q, k, v, qi, ki, wi, ga, gb = jnp.split(h @ w_in, SPLIT_POINTS, axis=-1)
    q = rope(q.reshape(B, S, N_HEADS, HEAD_DIM), pos)
    k = rope(k.reshape(B, S, N_KV_HEADS, HEAD_DIM), pos)
    v = v.reshape(B, S, N_KV_HEADS, HEAD_DIM)
    qi = rope(qi.reshape(B, S, N_IDX_HEADS, IDX_DIM), pos)
    ki = rope(ki[:, :, None, :], pos)[:, :, 0, :]
    wi = wi * IDX_W_SCALE
    return z_pool, q, k, v, qi, ki, wi, ga, gb

def pool_branch(z, n_out, w_pool, pool_scale):
    B, N, _ = z.shape
    zg = z.astype(jnp.float32).reshape(B, N, POOL_GROUPS, POOL_GROUP_DIM)
    cs = jnp.pad(jnp.cumsum(zg, axis=1), ((0, 0), (1, 0), (0, 0), (0, 0)))
    t = jnp.arange(N - n_out, N)
    outs = []
    for g, win in enumerate(POOL_WINDOWS):
        lo = jnp.maximum(t + 1 - win, 0)
        cnt = (t + 1 - lo).astype(jnp.float32)
        mean = (cs[:, t + 1, g] - cs[:, lo, g]) / cnt[None, :, None]
        outs.append(mean - zg[:, N - n_out:, g])
    d = jnp.stack(outs, axis=2)
    y = jnp.einsum('bngc,gcd->bngd', d, w_pool.astype(jnp.float32)).reshape(B, n_out, POOL_WIDTH)
    return (y * pool_scale.astype(jnp.float32)).astype(z.dtype)

def sparse_attention(q, qi, wi, q_chunk, k_all, v_all, ki_all, k_chunk, top_k):
    B, Q = q.shape[:2]
    sc = jnp.einsum('bqhd,bsd->bqhs', qi, ki_all, preferred_element_type=jnp.float32)
    score = jnp.einsum('bqhs,bqh->bqs', jax.nn.relu(sc), wi.astype(jnp.float32))
    admissible = k_chunk[None, :] <= q_chunk[:, None]
    score = jnp.where(admissible[None], score, -jnp.inf)
    _, idx = lax.top_k(score, top_k)
    valid = k_chunk[idx] <= q_chunk[None, :, None]
    k_sel = jax.vmap(lambda kb, ib: kb[ib])(k_all, idx)
    v_sel = jax.vmap(lambda vb, ib: vb[ib])(v_all, idx)
    qg = q.reshape(B, Q, N_KV_HEADS, KV_REP, HEAD_DIM)
    logits = jnp.einsum('bqgrd,bqkgd->bqgrk', qg, k_sel, preferred_element_type=jnp.float32) * ATTN_SCALE
    logits = jnp.where(valid[:, :, None, None, :], logits, -jnp.inf)
    p = jax.nn.softmax(logits, axis=-1)
    o = jnp.einsum('bqgrk,bqkgd->bqgrd', p.astype(v_sel.dtype), v_sel)
    return o.reshape(B, Q, Q_WIDTH)

def merge_branches(a, b, ga, gb, w_out):
    return (jax.nn.sigmoid(ga) * a + jax.nn.sigmoid(gb) * b) @ w_out

def token_mix_prompt(h, pos, w_in, w_pool, pool_scale, w_attn_out, w_out, top_k):
    B, N, _ = h.shape
    z_pool, q, k, v, qi, ki, wi, ga, gb = in_project(h, w_in, pos)
    a = pool_branch(z_pool, N, w_pool, pool_scale)
    k_chunk = chunk_index(pos)
    n_blk = -(-N // QUERY_BLOCK)
    pad = n_blk * QUERY_BLOCK - N

    def to_blocks(t):
        t = jnp.pad(t, [(0, 0), (0, pad)] + [(0, 0)] * (t.ndim - 2))
        return t.reshape((B, n_blk, QUERY_BLOCK) + t.shape[2:]).swapaxes(0, 1)

    q_chunk_blocks = chunk_index(jnp.arange(n_blk * QUERY_BLOCK)).reshape(n_blk, QUERY_BLOCK)

    def one_block(args):
        qb, qib, wib, qcb = args
        return sparse_attention(qb, qib, wib, qcb, k, v, ki, k_chunk, top_k)

    o = lax.map(one_block, (to_blocks(q), to_blocks(qi), to_blocks(wi), q_chunk_blocks))
    o = o.swapaxes(0, 1).reshape(B, n_blk * QUERY_BLOCK, Q_WIDTH)[:, :N]
    y = merge_branches(a, o @ w_attn_out, ga, gb, w_out)
    return y, k, v, ki, z_pool[:, N - POOL_STATE:]

def token_mix_sample(h, pos, cache_k, cache_v, cache_ki, state_pool, w_in, w_pool, pool_scale, w_attn_out, w_out, top_k):
    B, S, _ = h.shape
    z_pool, q, k, v, qi, ki, wi, ga, gb = in_project(h, w_in, pos)
    z_cat = jnp.concatenate([state_pool.astype(z_pool.dtype), z_pool], axis=1)
    a = pool_branch(z_cat, S, w_pool, pool_scale)
    k_all = jnp.concatenate([cache_k.astype(k.dtype), k], axis=1)
    v_all = jnp.concatenate([cache_v.astype(v.dtype), v], axis=1)
    ki_all = jnp.concatenate([cache_ki.astype(ki.dtype), ki], axis=1)
    k_chunk = chunk_index(jnp.arange(k_all.shape[1]))
    o = sparse_attention(q, qi, wi, chunk_index(pos), k_all, v_all, ki_all, k_chunk, top_k)
    y = merge_branches(a, o @ w_attn_out, ga, gb, w_out)
    return y, k, v, ki, z_cat[:, -POOL_STATE:]

def hier_moe(h, w_rg, b_rg, w_re, b_re, w_g, w_u, w_d):
    B, N, _ = h.shape
    g_logits = jnp.einsum('bnd,dg->bng', h, w_rg).astype(jnp.float32) + b_rg.astype(jnp.float32)
    g_sel = jnp.argmax(g_logits, axis=-1)
    g_prob = jnp.take_along_axis(jax.nn.softmax(g_logits, axis=-1), g_sel[..., None], axis=-1)
    e_logits = (jnp.einsum('bnd,de->bne', h, w_re).astype(jnp.float32) + b_re.astype(jnp.float32))
    e_logits = e_logits.reshape(B, N, N_EXPERT_GROUPS, EXPERTS_PER_GROUP)
    e_logits = jnp.take_along_axis(e_logits, g_sel[..., None, None], axis=2)[:, :, 0]
    top_v, top_i = lax.top_k(e_logits, EXPERT_TOPK)
    top_w = jax.nn.softmax(top_v, axis=-1) * g_prob
    within = jnp.einsum('bnk,bnke->bne', top_w, jax.nn.one_hot(top_i, EXPERTS_PER_GROUP, dtype=jnp.float32))
    comb = (jax.nn.one_hot(g_sel, N_EXPERT_GROUPS, dtype=jnp.float32)[..., None] * within[:, :, None, :])
    comb = comb.reshape(B, N, N_EXPERTS)
    act = jax.nn.silu(jnp.einsum('bnd,edf->bnef', h, w_g)) * jnp.einsum('bnd,edf->bnef', h, w_u)
    out = jnp.einsum('bnef,efd->bnd', act * comb.astype(act.dtype)[..., None], w_d)
    return out.astype(h.dtype)

def setup_inputs(seed: int = 0) -> dict:
    key = jax.random.key(seed)
    ks = jax.random.split(key, 22)

    def nrm(k, shape, scale=1.0):
        return jax.random.normal(k, shape, jnp.float32) * scale

    return {
        'x_prompt': nrm(ks[0], (BATCH, SEQ, D_MODEL)),
        'x_sample': nrm(ks[1], (DEC_BATCH, DEC_SEQ, D_MODEL)),
        'cache_k': nrm(ks[2], (DEPTH, DEC_BATCH, N_META + PAST_LEN, N_KV_HEADS, HEAD_DIM)),
        'cache_v': nrm(ks[3], (DEPTH, DEC_BATCH, N_META + PAST_LEN, N_KV_HEADS, HEAD_DIM)),
        'cache_idx_k': nrm(ks[4], (DEPTH, DEC_BATCH, N_META + PAST_LEN, IDX_DIM)),
        'state_pool': nrm(ks[5], (DEPTH, DEC_BATCH, POOL_STATE, POOL_WIDTH)),
        'meta_tokens': nrm(ks[6], (N_META, D_MODEL)),
        'norm_mix_g': 1.0 + nrm(ks[7], (DEPTH, D_MODEL), 0.01),
        'norm_ffn_g': 1.0 + nrm(ks[8], (DEPTH, D_MODEL), 0.01),
        'norm_final_g': 1.0 + nrm(ks[9], (D_MODEL,), 0.01),
        'w_in': nrm(ks[10], (DEPTH, D_MODEL, IN_WIDTH), D_MODEL ** -0.5),
        'w_pool': nrm(ks[11], (DEPTH, POOL_GROUPS, POOL_GROUP_DIM, POOL_GROUP_DIM), POOL_GROUP_DIM ** -0.5),
        'pool_scale': 1.0 + nrm(ks[12], (DEPTH, POOL_WIDTH), 0.01),
        'w_attn_out': nrm(ks[13], (DEPTH, Q_WIDTH, D_MODEL), Q_WIDTH ** -0.5),
        'w_out': nrm(ks[14], (DEPTH, D_MODEL, D_MODEL), D_MODEL ** -0.5),
        'w_router_group': nrm(ks[15], (DEPTH, D_MODEL, N_EXPERT_GROUPS), D_MODEL ** -0.5),
        'b_router_group': nrm(ks[16], (DEPTH, N_EXPERT_GROUPS), 0.01),
        'w_router_expert': nrm(ks[17], (DEPTH, D_MODEL, N_EXPERTS), D_MODEL ** -0.5),
        'b_router_expert': nrm(ks[18], (DEPTH, N_EXPERTS), 0.01),
        'w_expert_gate': nrm(ks[19], (DEPTH, N_EXPERTS, D_MODEL, D_EXPERT), D_MODEL ** -0.5),
        'w_expert_up': nrm(ks[20], (DEPTH, N_EXPERTS, D_MODEL, D_EXPERT), D_MODEL ** -0.5),
        'w_expert_down': nrm(ks[21], (DEPTH, N_EXPERTS, D_EXPERT, D_MODEL), D_EXPERT ** -0.5),
    }

def reference(x_prompt, x_sample, cache_k, cache_v, cache_idx_k, state_pool, meta_tokens,
              norm_mix_g, norm_ffn_g, norm_final_g, w_in, w_pool, pool_scale, w_attn_out, w_out,
              w_router_group, b_router_group, w_router_expert, b_router_expert,
              w_expert_gate, w_expert_up, w_expert_down):
    B, seq = x_prompt.shape[:2]
    dec = x_sample.shape[1]
    past = cache_k.shape[2] - N_META
    top_k_prompt = min(IDX_TOPK, seq // 4)
    top_k_sample = min(IDX_TOPK, (past + dec) // 4)
    xp = jnp.concatenate([jnp.broadcast_to(meta_tokens.astype(x_prompt.dtype)[None], (B, N_META, D_MODEL)), x_prompt], axis=1)
    xs = x_sample
    pos_p = jnp.arange(N_META + seq)
    pos_s = N_META + past + jnp.arange(dec)
    kp_l, vp_l, kip_l, pp_l, ks_l, vs_l, kis_l, ps_l = [], [], [], [], [], [], [], []
    for l in range(DEPTH):
        yp, kp, vp, kip, pp = token_mix_prompt(rms_norm(xp, norm_mix_g[l]), pos_p, w_in[l], w_pool[l], pool_scale[l],
                                               w_attn_out[l], w_out[l], top_k_prompt)
        xp = xp + yp
        xp = xp + hier_moe(rms_norm(xp, norm_ffn_g[l]), w_router_group[l], b_router_group[l], w_router_expert[l],
                           b_router_expert[l], w_expert_gate[l], w_expert_up[l], w_expert_down[l])
        ys, ks_, vs_, kis, ps = token_mix_sample(rms_norm(xs, norm_mix_g[l]), pos_s, cache_k[l], cache_v[l], cache_idx_k[l],
                                                 state_pool[l], w_in[l], w_pool[l], pool_scale[l], w_attn_out[l], w_out[l],
                                                 top_k_sample)
        xs = xs + ys
        xs = xs + hier_moe(rms_norm(xs, norm_ffn_g[l]), w_router_group[l], b_router_group[l], w_router_expert[l],
                           b_router_expert[l], w_expert_gate[l], w_expert_up[l], w_expert_down[l])
        kp_l.append(kp); vp_l.append(vp); kip_l.append(kip); pp_l.append(pp)
        ks_l.append(ks_); vs_l.append(vs_); kis_l.append(kis); ps_l.append(ps)
    y_prompt = rms_norm(xp[:, N_META:], norm_final_g)
    y_sample = rms_norm(xs, norm_final_g)
    k_prompt = jnp.stack(kp_l)
    v_prompt = jnp.stack(vp_l)
    idx_k_prompt = jnp.stack(kip_l)
    pool_prompt = jnp.stack(pp_l)
    k_sample = jnp.stack(ks_l)
    v_sample = jnp.stack(vs_l)
    idx_k_sample = jnp.stack(kis_l)
    pool_sample = jnp.stack(ps_l)
    return (y_prompt, y_sample, k_prompt, v_prompt, idx_k_prompt, pool_prompt, k_sample, v_sample, idx_k_sample, pool_sample)


_drawn_inputs = setup_inputs


def setup_inputs(seed=0):
    import zlib

    import numpy as np

    out = dict(_drawn_inputs(seed))
    spreads = {}
    factors = {}
    for name, (base, spread) in spreads.items():
        noise = np.random.default_rng([zlib.crc32(name.encode()), seed]).standard_normal(out[name].shape)
        drawn = base * np.exp(spread * noise) if base else spread * noise
        out[name] = jnp.asarray(drawn.astype(out[name].dtype))
    for name, factor in factors.items():
        out[name] = (out[name] * factor).astype(out[name].dtype)
    return out
```

```python
import math
from contextlib import ExitStack

import numpy as np

import concourse.bass as bass
from concourse import mybir

F32 = mybir.dt.float32
BF16 = mybir.dt.bfloat16
I32 = mybir.dt.int32
U32 = mybir.dt.uint32
ALU = mybir.AluOpType
ACT = mybir.ActivationFunctionType
AX = mybir.AxisListType

P = 128
D = 1024
KD = D // P
META = 16
SEQ = 1024
DEC_B, DEC_S = 8, 16
PAST = 512
CHUNK = 64
NPT = SEQ // P
NT = NPT + 1
COLS = META + SEQ + DEC_B * DEC_S
TOK = COLS - META
SAMPLE0 = META + SEQ
EPS = 1e-6
HEADS, KVH, HD, REP = 8, 2, 128, 4
IH, ID = 4, 64
TOPK_P = 256
TOPK_S = (PAST + DEC_S) // 4
CACHE = META + PAST
SK = CACHE + DEC_S
ATTN_SCALE = HD ** -0.5
IDX_SCALE = (IH * ID) ** -0.5
POOL_STATE = 15
C_Z, C_Q, C_KV, C_IDX, C_GA, C_GB = 0, 1024, 2048, 2560, 2884, 3908
IDXW = IH * ID + ID + IH
NE, DE = 32, 128
NG, EPG = 4, 8
MAX_OVER = 2 * TOK // P
OVER_J = TOK // P - 1
MASKED = -3.0e38
TAKEN = -3.4e38
BETWEEN = -3.2e38
NEG_BIAS = -1.0e30

K_ID, K_ROPE, K_I32, K_BASE, K_I4, K_SI, K_THR = 0, 128, 128 + 480, 640, 672, 676, 677
K_END = K_THR + OVER_J


def splits(n, most=512):
    k = -(-n // most)
    w = -(-n // k)
    return [(c, min(c + w, n)) for c in range(0, n, w)]


def build(nc, a):
    ctx = ExitStack()
    with ctx:
        def sb(name, shape, dt=F32):
            return ctx.enter_context(nc.sbuf_tensor(name, shape, dt))

        def sem(name):
            return ctx.enter_context(nc.semaphore(name))

        def sems(name, n):
            return [sem(f"{name}{i}") for i in range(n)]

        RH = sb("region_h", [P, 9344])
        RW = sb("region_w", [P, 8192])
        RQ = sb("region_q", [P, 9216])
        RK = sb("region_kv", [P, 10240])
        RT = sb("region_t", [P, 12080])
        consts = sb("consts", [P, K_END])
        cbf_raw = sb("cbf", [P, 10 * P], mybir.dt.uint16)
        tokid = sb("tokid", [P, NT], I32)
        nbuf = sb("nbuf", [P, 3, 512])
        small = sb("small", [P, 528])

        def view(r, off, *dims):
            n = int(np.prod(dims))
            v = r[:, off:off + n]
            if len(dims) == 2:
                v = v.rearrange("p (a b) -> p a b", a=dims[0])
            if len(dims) == 3:
                v = v.rearrange("p (a b c) -> p a b c", a=dims[0], b=dims[1])
            return v

        sm_at = [0]

        def sm(*dims):
            off = sm_at[0]
            sm_at[0] += int(np.prod(dims))
            assert sm_at[0] <= 528
            return view(small, off, *dims)

        cbf = cbf_raw[:, :].bitcast(BF16)
        ident = consts[:, K_ID:K_ID + P]
        ropec = consts[:, K_ROPE:K_ROPE + 480].rearrange("p (t c) -> p t c", t=10)
        iota32 = consts[:, K_I32:K_I32 + NE]
        base32 = consts[:, K_BASE:K_BASE + NE]
        iota4 = consts[:, K_I4:K_I4 + NG]
        siota = consts[:, K_SI:K_SI + 1]
        overthr = consts[:, K_THR:K_THR + OVER_J]
        repb = cbf[:, 0:8 * P].rearrange("p (b m) -> p b m", b=8)
        upper = cbf[:, 8 * P:9 * P]
        onesb = cbf[:, 9 * P:10 * P]

        gmix = sm(KD)
        pscale = sm(KD)
        wis = sm(10, IH)
        rbias = sm(NG + NE)
        wrout = sm(KD, NG + NE)
        mx3 = sm(8, 3)
        mx1 = sm(8)
        nmx = sm(8)
        rsum = sm(8)
        rinv = sm(8)
        m8 = sm(2, 8)
        tnrm = sm(NT, 2)
        wts = sm(NT, 2)
        fnrm = sm(NT, 2)
        mhalf = sm(1)
        vjunk = sm(1)
        pjunk = sm(1)
        assert sm_at[0] <= 528
        ypos = sb("ypos", [P, NT, 2], I32)
        posi = sb("posi", [P, NT, 2], I32)
        lidx = sb("lidx", [P, NE], I32)
        over_i = sb("over_i", [P, 2], I32)
        over_row = sb("over_row", [1, 32], I32)
        lidx_o = sb("lidx_o", [P, 1], I32)

        hT = view(RH, 0, KD, COLS)
        sq = view(RT, 0, 2, COLS)
        rbc = view(RT, 2 * COLS, COLS)
        ones_f = view(RT, 3 * COLS, P)
        zero_i = RQ[:, 8400:8400 + NE * TOK // P].bitcast(I32)
        rope_t = RT[:, 1536:2048].rearrange("p (n q c) -> p n q c", n=2, q=4)
        wslot = [view(RW, 0, KD, 512), view(RW, 4096, KD, 512)]
        qiT = view(RQ, 0, 2, SEQ)
        kiT = view(RQ, 2048, SEQ + META)
        qiB = view(RQ, 3088, IH, 640)
        kiC = view(RQ, 3088 + 2560, 4, SK)
        idxd = view(RQ, 7824, IH, 2, ID)
        rel = view(RT, 0, 3, 512)
        vS = view(RK, 0, 10, 256)
        kT = view(RK, 2560, KVH, COLS)
        n_keys = [META + P * (i + 1) for i in range(NPT)]
        s_off = [4896 + sum(n_keys[:i]) for i in range(NPT)]
        sc = [RK[:, s_off[i]:s_off[i] + n_keys[i]] for i in range(NPT)]
        s_off_s = s_off[-1] + n_keys[-1]
        assert s_off_s + SK + 4 <= 10240
        sc_s = RK[:, s_off_s:s_off_s + SK + 4]
        qT = view(RQ, 0, HEADS, TOK)
        zT = view(RT, 0, 2, COLS)
        wa, wb = view(RT, 2336, COLS), view(RT, 3504, COLS)
        za, zb = view(RT, 4672, DEC_B, 31), view(RT, 4920, DEC_B, 31)
        dT = view(RT, 5168, 2, TOK)
        sg = view(RT, 7472, 2, TOK)
        ub = view(RT, 9776, 2, TOK)
        nflat = nbuf[:, :, :].rearrange("p a b -> p (a b)")
        wpool = nflat[:, 0:1024].rearrange("p (g k d) -> p g k d", g=2, k=2)
        zs = nflat[:, 1024:1520].rearrange("p (a b c) -> p a b c", a=2, b=DEC_B)
        sbias = sb("sbias", [P, SK], BF16)
        PB = [view(RT, 0, REP, 1040), view(RT, 4160, REP, 1040)]
        PT = view(RT, 8320, 4, 512)
        kTb = view(RH, 0, 3, KVH * SK)
        vb = view(RH, 3 * KVH * SK, 3, 5 * 256)
        zero = RH[:, 7104:7104 + 272]
        qsb = view(RH, 7376, 3, HEADS * DEC_S)
        wao = [view(RW, 0, 4, D), view(RW, 4096, 4, D)]
        mT = view(RH, 0, KD, TOK)
        wout = view(RT, 0, KD, D)
        sB = view(RT, 8192, 2, TOK)
        mtmp = view(RT, 10496, 3, 384)
        x2 = view(RK, 0, NT, D)
        gffn = RK[:, 9216:10240]
        h2 = view(RT, 8192, 2, D)
        h2T = view(RT, 10240, KD, P)
        rt = RT[:, 11264:12080]
        eslot = ([RW[:, 0:3072], RW[:, 3072:6144]] + [RQ[:, 3072 * i:3072 * i + 3072] for i in range(3)]
                 + [RH[:, 3072 * i:3072 * i + 3072] for i in range(3)])
        NSLOT = len(eslot)

        def e_gate(s):
            return eslot[s][:, 0:1024].rearrange("p (k f) -> p k f", k=KD)

        def e_up(s):
            return eslot[s][:, 1024:2048].rearrange("p (k f) -> p k f", k=KD)

        def e_down(s):
            return eslot[s][:, 2048:3072]

        hg = view(RT, 0, 3, D)
        hgT = view(RT, 3072, 2, KD, P)
        silu = view(RT, 5120, 2, P)
        actT = view(RT, 5376, 2, P)
        ysb = view(RT, 5632, 3, D)
        ya = view(RT, 8704, 2, D)
        yb = view(RT, 3072, 2, D)
        gfin = RT[:, 10752:11776]

        r_at = [0]

        def rtile(*dims, dt=None):
            n = int(np.prod(dims)) // (2 if dt == BF16 else 1)
            v = rt[:, r_at[0]:r_at[0] + n]
            r_at[0] += n
            assert r_at[0] <= 816
            if dt is not None:
                v = v.bitcast(dt)
            return v if len(dims) == 1 else v.rearrange("p (a b) -> p a b", a=dims[0])

        r_lg = rtile(40)
        r_m8g = rtile(8)
        r_i8g = rtile(8, dt=U32)
        r_ngm = rtile(1)
        r_gsel = rtile(1)
        r_gexp = rtile(4)
        r_gs = rtile(1)
        r_mk = rtile(4)
        r_mk2 = rtile(4)
        r_em = rtile(NG, EPG)
        r_emf = r_em.rearrange("p a b -> p (a b)")
        r_m8e = rtile(8)
        r_i8e = rtile(8, dt=U32)
        r_dv = rtile(1)
        r_ex = rtile(1)
        r_den = rtile(1)
        r_rb = rtile(NE)
        r_junk = rtile(2, NE)
        r_oh = nflat[:, 0:NT * 2 * NE].rearrange("p (t e) -> p t e", t=NT)
        r_if = rtile(NT, 2)
        r_rank = rtile(NT, 2)
        r_sel = rtile(NT, 2)
        r_y1 = rtile(NT, 2)
        r_y2 = rtile(NT, 2)
        onehots = rtile(NT + 1, NE, dt=BF16)
        a_bf = rtile(NT, NE, dt=BF16)
        r_pos = rtile(2)
        f_flag = view(RT, 8192, NE, OVER_J)
        f_cum = view(RT, 8192 + NE * OVER_J, NE * OVER_J)
        f_one = view(RT, 8192 + 2 * NE * OVER_J, NE * OVER_J)
        f_junk = view(RT, 8192 + 3 * NE * OVER_J, NE * OVER_J)
        f_id = view(RT, 8192 + 4 * NE * OVER_J, 1)
        f_ob = view(RT, 8200 + 4 * NE * OVER_J, NE)

        bank = [ctx.enter_context(nc.psum_tensor(f"bank{i}", [P, 512], F32)) for i in range(8)]

        uA_d = nc.dram_tensor("gated_pool_scratch", (KD, P, TOK), F32, kind="Internal").ap()
        sB_d = nc.dram_tensor("gate_b_scratch", (KD, P, TOK), F32, kind="Internal").ap()
        h2_d = nc.dram_tensor("ffn_input_scratch", (TOK, D), F32, kind="Internal").ap()
        y_d = nc.dram_tensor("expert_rows_scratch", ((NE + MAX_OVER) * P, D), F32, kind="Internal").ap()
        list_d = nc.dram_tensor("expert_lists_scratch", (NE * TOK, 1), I32, kind="Internal").ap()
        over_d = nc.dram_tensor("overflow_table_scratch", (32, 1), I32, kind="Internal").ap()

        NAT = ([("idx", t) for t in range(10)] + [("kv", t) for t in range(10)]
               + [("q0", t) for t in range(1, 10)] + [("q1", t) for t in range(1, 10)])
        N_IDX, N_KV = 10, 20
        N_NAT = len(NAT)
        TR_N = [2 if nt == ("idx", 9) else 1 for nt in NAT]
        TR_AT = [sum(TR_N[:n]) for n in range(N_NAT + 1)]
        TOK3 = [(0, 384), (384, 768), (768, 1152)]
        COL3 = [(0, 400), (400, 784), (784, COLS)]

        def u_z(g, cc):
            return N_NAT + 18 * g + 3 * cc

        def u_ga(g, cc):
            return N_NAT + 18 * g + 6 + 3 * cc

        def u_pool(g, cc):
            return N_NAT + 18 * g + 12 + 3 * cc

        def u_gb(c):
            return N_NAT + 72 + 3 * c

        W_LAST = [N_IDX, N_KV, N_KV + NT, N_NAT] + [u_ga(g, 1) + 3 for g in range(4)] + [u_gb(4), u_gb(8)]

        def tcols(tt):
            if tt == 0:
                return 0, META
            return META + P * (tt - 1), P

        SCU = [(i, c, h) for i in range(1, NPT) for c in splits(n_keys[i]) for h in range(IH)]
        SCU += [(8, c, h) for c in splits(SK) for h in range(IH)]
        SEL_ORDER = [0, 1, 2, 3, 4, 5, 6, 8, 7]

        AG = [("p", i, g) for i in range(NPT) for g in range(KVH)] + [("s", b, 0) for b in range(DEC_B)]

        def heads_of(G):
            return REP if AG[G][0] == "p" else 1

        def chunks_of(G):
            return splits(n_keys[AG[G][1]]) if AG[G][0] == "p" else splits(SK)

        def trs_of(G):
            return AG[G][1] + 2 if AG[G][0] == "p" else 2

        U_AT = [sum(heads_of(x) for x in range(G)) for G in range(len(AG) + 1)]
        S_AT = [sum(heads_of(x) * len(chunks_of(x)) for x in range(G)) for G in range(len(AG) + 1)]
        T_AT = [sum(trs_of(x) for x in range(G)) for G in range(len(AG) + 1)]

        x_in = sems("x_in", KD)
        const_in = sem("const_in")
        sq_ready = sem("sq_ready")
        sq_used = sem("sq_used")
        r_ready = sem("mean_square_plus_eps")
        root_ready = sem("root_ready")
        rstd_ready = sem("rstd_ready")
        frstd_ready = sem("final_rstd_ready")
        h_ready = sem("h_ready")
        ones_ready = sem("ones_ready")
        w_in_s = sems("w_loaded", 12)
        wp_in = sems("w_pool_in", 2)
        pj_done = sem("proj_done")
        pj_evac = sem("proj_evacuated")
        tr_done = sem("transposed")
        tr_evac = sem("transposed_evacuated")
        rope_done = sem("rope_done")
        nat_out = sems("nat_out", 3)
        v_out = sem("v_out")
        qib_zero = sem("qib_zero")
        kic_in = sem("kic_in")
        sc_done = sem("score_done")
        sc_relu = sem("score_relu")
        sc_acc = sem("score_accumulated")
        selected = sem("selected")
        dve_c = sem("dve_chain")
        act_c = sem("act_chain")
        pool_c = sem("pool_chain")
        st_in = sems("pool_state_in", 2)
        win_done = sem("windows_done")
        pool_out = sems("pool_rows_out", 2)
        u_done = sem("gated_pool_done")
        u_out = sems("gated_pool_out", 2)
        sb_out = sems("gate_b_out", 2)
        kb_in = sems("cache_in", 3)
        kb_new = sem("cache_new_keys")
        zero_ready = sem("zero_ready")
        a_s = sem("logits_done")
        a_sm = sem("logits_taken")
        a_max = sem("max_ready")
        a_exp = sem("exp_done")
        a_ri = sem("inverse_sum_ready")
        a_p = sem("probs_ready")
        a_t = sem("probs_transposed")
        a_te = sem("probs_transposed_evacuated")
        a_o = sem("head_output_done")
        a_oe = sem("head_output_evacuated")
        mu_in = sems("gated_pool_in", KD)
        sbi_in = sems("gate_b_in", 2)
        wo_in = sem("w_out_in")
        b6_done = sem("attn_out_done")
        b6_evac = sem("attn_out_evacuated")
        m_ready = sem("merged_ready")
        x2_in = sems("x2_in", NT)
        g2_in = sem("gffn_in")
        o7_done = sem("out_proj_done")
        x2_ready = sem("x2_ready")
        ms_ready = sem("mean_square_ready")
        h2_ready = sem("h2_ready")
        h2_out = sems("h2_out", 2)
        t7_done = sem("h2_transposed")
        t7_evac = sem("h2_transposed_evacuated")
        lg_done = sem("router_logits_done")
        gexp_in = sem("group_exp_wanted")
        gexp_done = sem("group_exp_done")
        eexp_in = sem("expert_exp_wanted")
        eexp_done = sem("expert_exp_done")
        hot_ready = sem("onehot_ready")
        rank_done = sem("rank_done")
        pos_ready = sem("positions_ready")
        y_init = sem("overflow_rows_initialised")
        ypos_ready = sem("row_positions_ready")
        list_init = sem("lists_initialised")
        scattered = sem("lists_scattered")
        cnt_done = sem("counts_done")
        over_ready = sem("overflow_table_ready")
        over_out = sem("overflow_table_out")
        over_in = sem("overflow_table_in")
        lidx_in = sem("list_heads_in")
        ew_in = sems("expert_weights_in", NSLOT)
        hg_in = sems("rows_gathered", 3)
        te_done = sem("rows_transposed")
        te_evac = sem("rows_transposed_evacuated")
        gu_done = sem("gate_up_done")
        silu_done = sem("silu_done")
        act_ready = sem("act_ready")
        dn_done = sem("down_done")
        y_ready = sem("y_ready")
        y_out = sems("y_out", 3)
        ov_w = sem("over_weights_in")
        ov_l = sem("over_list_in")
        ov_h = sem("over_rows_in")
        ov_y = sem("over_y_out")
        gfin_in = sem("gfin_in")
        ya_in = sems("ya_in", 2)
        yb_in = sems("yb_in", 2)
        y1_done = sem("row_sum_done")
        fms_ready = sem("final_mean_square_ready")
        fin_ready = sem("final_ready")
        fin_out = sem("final_out")

        block = ctx.enter_context(nc.Block())

        w_v = a["w_in"].rearrange("(k p) n -> p k n", p=P)

        @block.sync
        def _(sp):
            for k in range(KD):
                sp.dma_start(hT[:, k, :], a["xT"][k * P:(k + 1) * P, :]).then_inc(x_in[k], 16)
            sp.dma_start(gmix, a["gmix"]).then_inc(const_in, 16)
            sp.dma_start(pscale, a["pscale"]).then_inc(const_in, 16)
            sp.dma_start(consts[:, :], a["consts"]).then_inc(const_in, 16)
            sp.dma_start(cbf_raw[:, :], a["cbf"]).then_inc(const_in, 16)
            sp.dma_start(tokid[:, :], a["tokid"]).then_inc(const_in, 16)
            sp.dma_start(rbias, a["rbias"]).then_inc(const_in, 16)
            sp.dma_start(wrout, a["wrout"].rearrange("(k p) e -> p k e", p=P)).then_inc(const_in, 16)

            def load_w(n):
                if n >= 2:
                    sp.wait_ge(pj_done, W_LAST[n - 2])
                s = wslot[n % 2]
                if n < 4:
                    c0 = [C_IDX, C_KV, C_Q, C_Q + 512][n]
                    wd = IDXW if n == 0 else 512
                    sp.dma_start(s[:, :, 0:wd], w_v[:, :, c0:c0 + wd]).then_inc(w_in_s[n], 16)
                elif n < 8:
                    g = n - 4
                    sp.dma_start(s[:, :, 0:256], w_v[:, :, C_Z + 256 * g:C_Z + 256 * g + 256]).then_inc(w_in_s[n], 16)
                    sp.dma_start(s[:, :, 256:512], w_v[:, :, C_GA + 256 * g:C_GA + 256 * g + 256]).then_inc(w_in_s[n], 16)
                elif n < 10:
                    c0 = C_GB + 512 * (n - 8)
                    sp.dma_start(s[:, :, :], w_v[:, :, c0:c0 + 512]).then_inc(w_in_s[n], 16)
                else:
                    h0 = 4 * (n - 10)
                    src = a["w_attn_out"].rearrange("(k p) n -> p k n", p=P)
                    sp.dma_start(wao[n - 10], src[:, h0:h0 + 4, :]).then_inc(w_in_s[n], 16)

            load_w(0)
            load_w(1)
            sp.dma_start(kiC[:, :, 0:CACHE], a["kiC"].rearrange("q p s -> p q s")).then_inc(kic_in, 16)

            def out_nat(n):
                kind, tt = NAT[n]
                sp.wait_ge(rope_done, n + 1)
                c0, rows = tcols(tt)
                if kind == "idx":
                    src = nbuf[0:rows, n % 3, 256:320]
                    dst = a["o_ki"][c0:c0 + rows, :] if tt < 9 else a["o_kis"]
                    sp.dma_start(dst, src).then_inc(nat_out[n % 3], 16)
                else:
                    src = nbuf[0:rows, n % 3, 0:256]
                    dst = a["o_k"][c0:c0 + rows, :] if tt < 9 else a["o_ks"]
                    sp.dma_start(dst, src).then_inc(nat_out[n % 3], 16)
                    dst = a["o_v"][c0:c0 + rows, :] if tt < 9 else a["o_vs"]
                    sp.dma_start(dst, vS[0:rows, tt, :]).then_inc(v_out, 16)

            for n in range(N_IDX):
                out_nat(n)
            load_w(2)
            for n in range(N_IDX, N_KV):
                out_nat(n)
            load_w(3)
            load_w(4)
            load_w(5)

            def state_in(zi):
                if zi >= 2:
                    sp.wait_ge(win_done, zi - 1)
                    sp.wait_ge(pool_out[zi % 2], 32 * (zi // 2))
                else:
                    sp.wait_ge(tr_done, TR_AT[N_NAT])
                sp.dma_start(zs[:, zi % 2, :, 0:15],
                             a["stateT"][:, zi * P:(zi + 1) * P, :].rearrange("b p s -> p b s")).then_inc(st_in[zi % 2], 16)

            def pool_rows(zi):
                sp.wait_ge(win_done, zi + 1)
                sp.dma_start(a["o_poolT"][zi * P:(zi + 1) * P, :],
                             zT[:, zi % 2, SAMPLE0 - POOL_STATE:SAMPLE0]).then_inc(pool_out[zi % 2], 16)
                sp.dma_start(a["o_poolsT"][:, zi * P:(zi + 1) * P, :].rearrange("b p s -> p b s"),
                             zs[:, zi % 2, :, 16:31]).then_inc(pool_out[zi % 2], 16)

            state_in(0)
            state_in(1)
            for g in range(4):
                for cc in range(2):
                    zi = 2 * g + cc
                    pool_rows(zi)
                    if zi + 2 < KD:
                        state_in(zi + 2)
                for cc in range(2):
                    c = 2 * g + cc
                    sp.wait_ge(u_done, c + 1)
                    sp.dma_start(uA_d[c, :, :], ub[:, c % 2, :]).then_inc(u_out[c % 2], 16)
                if g < 3:
                    load_w(6 + g)
            load_w(9)
            for c in range(KD):
                sp.wait_ge(pj_evac, u_gb(c) + 3)
                sp.dma_start(sB_d[c, :, :], sg[:, c % 2, :]).then_inc(sb_out[c % 2], 16)
            load_w(10)
            load_w(11)

            def cache_in(b):
                if b >= 3:
                    sp.wait_ge(a_o, 2 * NPT + b - 2)
                s = b % 3
                v = vb[:, s, :].rearrange("p (j d) -> p j d", j=5)
                kt = kTb[:, s, :].rearrange("p (g n) -> p g n", g=KVH)
                sp.dma_start(kt[:, :, 0:CACHE], a["ckT"][b].rearrange("g d s -> d g s")).then_inc(kb_in[s], 16)
                sp.dma_start(v[:, 0:4, :], a["cv"][b, 0:512, :].rearrange("(j p) d -> p j d", p=P)).then_inc(kb_in[s], 16)
                sp.dma_start(v[0:16, 4, :], a["cv"][b, 512:CACHE, :]).then_inc(kb_in[s], 16)
                sp.dma_start(v[16:32, 4, :], vS[16 * b:16 * b + 16, 9, :]).then_inc(kb_in[s], 16)

            sp.wait_ge(pj_done, u_gb(KD))
            for b in range(DEC_B):
                cache_in(b)
                if b == 2:
                    sp.wait_ge(zero_ready, 1)
                    sp.dma_start(y_d[NE * P:(NE + MAX_OVER) * P, :].rearrange("(p r) (s c) -> p (r s) c", p=P, c=256),
                                 zero[:, 0:256].unsqueeze(1).to_broadcast([P, MAX_OVER * D // 256, 256])).then_inc(y_init, 16)
            sp.wait_ge(a_oe, len(AG))
            sp.wait_ge(y_init, 16)
            for s in range(2):
                sp.wait_ge(u_out[s], 64)
                sp.wait_ge(sb_out[s], 64)
            for c in range(KD):
                sp.dma_start(mT[:, c, :], uA_d[c, :, :]).then_inc(mu_in[c], 16)
                if c < 2:
                    sp.dma_start(sB[:, c, :], sB_d[c, :, :]).then_inc(sbi_in[c], 16)
            w_o = a["w_out"].rearrange("(k p) n -> p k n", p=P)
            for c in range(2, KD):
                sp.wait_ge(b6_evac, 3 * (c - 1))
                sp.dma_start(sB[:, c % 2, :], sB_d[c, :, :]).then_inc(sbi_in[c % 2], 16)
                if c == 2:
                    sp.dma_start(wout, w_o).then_inc(wo_in, 16)
                    for t in range(NT):
                        src = a["x"][t * P:(t + 1) * P, :]
                        sp.dma_start(x2[:, t, :], src).then_inc(x2_in[t], 16)
                    sp.dma_start(gffn, a["gffn"]).then_inc(g2_in, 16)

            def load_e(e):
                s = e % NSLOT
                sp.dma_start(e_gate(s), a["wg"][e].rearrange("(k p) f -> p k f", p=P)).then_inc(ew_in[s], 16)
                sp.dma_start(e_up(s), a["wu"][e].rearrange("(k p) f -> p k f", p=P)).then_inc(ew_in[s], 16)
                sp.dma_start(e_down(s), a["wd"][e]).then_inc(ew_in[s], 16)

            sp.wait_ge(b6_done, 24)
            for e in range(5):
                load_e(e)
            for t in range(NT):
                sp.wait_ge(h2_ready, t + 1)
                sp.dma_start(h2_d[t * P:(t + 1) * P, :], h2[:, t % 2, :]).then_inc(h2_out[t % 2], 16)
            sp.wait_ge(o7_done, 2 * NT)
            for e in range(5, NSLOT):
                load_e(e)
            sp.wait_ge(over_ready, 1)
            sp.dma_start(over_d[0:MAX_OVER, :], over_i[0:MAX_OVER, 0:1]).then_inc(over_out, 16)
            sp.dma_start(over_d[31:32, :], over_i[0:1, 1:2]).then_inc(over_out, 16)
            sp.wait_ge(over_out, 32)
            sp.dma_start(over_row[0:1, 0:MAX_OVER], over_d.rearrange("n o -> o n")[:, 0:MAX_OVER]).then_inc(over_in, 16)
            sp.dma_start(over_row[0:1, 31:32], over_d.rearrange("n o -> o n")[:, 31:32]).then_inc(over_in, 16)
            sp.wait_ge(scattered, 16 * 2 * NT)
            sp.dma_start(lidx[:, :], list_d.rearrange("(e s) o -> s (e o)", e=NE)[0:P, :],
                         allow_slow_non_contiguous=True).then_inc(lidx_in, 16)
            for e in range(NE):
                sp.wait_ge(y_ready, e + 1)
                sp.dma_start(y_d[e * P:(e + 1) * P, :], ysb[:, e % 3, :]).then_inc(y_out[e % 3], 16)
                if e + NSLOT < NE:
                    sp.wait_ge(dn_done, e + 1)
                    load_e(e + NSLOT)
            sp.dma_start(gfin, a["gfin"]).then_inc(gfin_in, 16)
            for t in range(NT):
                sp.wait_ge(fin_ready, t + 1)
                dst = a["o_y"][t * P:(t + 1) * P, :] if t < NPT else a["o_ys"]
                sp.dma_start(dst, x2[:, t, :]).then_inc(fin_out, 16)
            sp.wait_ge(fin_out, 16 * NT)
            for s in range(3):
                sp.wait_ge(nat_out[s], 16 * len([n for n in range(N_KV) if n % 3 == s]))
            sp.wait_ge(v_out, 160)
            for s in range(2):
                sp.wait_ge(pool_out[s], 128)

        @block.tensor
        def _(pe):
            mm = nc.tensor.matmul
            pe.wait_ge(ones_ready, 1)
            for k in range(KD):
                pe.wait_ge(sq_ready, k + 1)
                for j, (c0, c1) in enumerate(COL3):
                    last = mm(bank[j][:, 0:c1 - c0], ones_f, sq[:, k % 2, c0:c1],
                              start=(k == 0), stop=(k == KD - 1))
                last.then_inc(sq_used, 1)

            def proj_nat(n):
                kind, tt = NAT[n]
                w = {"idx": 0, "kv": 1, "q0": 2, "q1": 3}[kind]
                if n == 0:
                    pe.wait_ge(h_ready, KD)
                if n == 0 or NAT[n - 1][0] != kind:
                    pe.wait_ge(w_in_s[w], 16)
                if n >= 4:
                    pe.wait_ge(pj_evac, n - 3)
                c0, rows = tcols(tt)
                wd = IDXW if kind == "idx" else 512
                for k in range(KD):
                    last = mm(bank[n % 4][0:rows, 0:wd], hT[:, k, c0:c0 + rows], wslot[w % 2][:, k, 0:wd],
                              start=(k == 0), stop=(k == KD - 1))
                last.then_inc(pj_done, 1)

            def trans_nat(n):
                kind, tt = NAT[n]
                rows = tcols(tt)[1]
                pe.wait_ge(rope_done, n + 1)
                v = TR_AT[n]
                if v >= 2:
                    pe.wait_ge(tr_evac, v - 1)
                b = bank[4 + v % 2]
                src = nbuf[0:rows, n % 3, :]
                idn = ident[0:rows, 0:rows]
                if kind == "idx" and tt == 0:
                    last = nc.tensor.transpose(b[:, 0:rows], src[:, 256:384], idn)
                elif kind == "idx" and tt < 9:
                    for j in range(3):
                        last = nc.tensor.transpose(b[:, j * P:(j + 1) * P], src[:, j * P:(j + 1) * P], idn)
                elif kind == "idx":
                    for j in range(4):
                        last = nc.tensor.transpose(b[:, j * P:(j + 1) * P],
                                                   idxd[:, j, :, :].rearrange("p u d -> p (u d)"), idn)
                    last.then_inc(tr_done, 1)
                    pe.wait_ge(tr_evac, v)
                    last = nc.tensor.transpose(bank[4 + (v + 1) % 2][:, 0:P], src[:, 256:384], idn)
                elif kind == "kv":
                    for j in range(2):
                        last = nc.tensor.transpose(b[:, j * P:j * P + rows], src[:, j * P:(j + 1) * P], idn)
                else:
                    for j in range(4):
                        last = nc.tensor.transpose(b[:, j * P:(j + 1) * P], src[:, j * P:(j + 1) * P], idn)
                last.then_inc(tr_done, 1)

            def nat_group(lo, hi):
                for n in range(lo, hi + 2):
                    if n < hi:
                        proj_nat(n)
                    if n - 2 >= lo:
                        trans_nat(n - 2)

            nat_group(0, N_IDX)
            pe.wait_ge(tr_evac, TR_AT[N_IDX])
            pe.wait_ge(kic_in, 16)
            for s, (i, (c0, c1), h) in enumerate(SCU):
                if s >= 2:
                    pe.wait_ge(sc_relu, s - 1)
                b = bank[6 + s % 2][:, 0:c1 - c0]
                if i < 8:
                    o = ID * (h % 2)
                    last = mm(b, qiT[o:o + ID, h // 2, i * P:(i + 1) * P], kiT[o:o + ID, c0:c1], start=True, stop=True)
                else:
                    for q in range(4):
                        last = mm(b, qiB[:, h, q * P:(q + 1) * P], kiC[:, q, c0:c1], start=(q == 0), stop=(q == 3))
                last.then_inc(sc_done, 1)
            nat_group(N_IDX, N_KV)
            nat_group(N_KV, N_NAT)

            def proj_t(u, w, lhs, rhs, n):
                pe.wait_ge(pj_evac, u - 3)
                for k in range(n):
                    last = mm(bank[u % 4][:, 0:rhs(k).shape[-1]], lhs(k), rhs(k), start=(k == 0), stop=(k == n - 1))
                last.then_inc(pj_done, 1)

            wp_v = wpool
            for g in range(4):
                ws = wslot[g % 2]
                pe.wait_ge(w_in_s[4 + g], 32)
                for cc in range(2):
                    for j, (c0, c1) in enumerate(COL3):
                        proj_t(u_z(g, cc) + j, 4 + g, lambda k: ws[:, k, cc * P:(cc + 1) * P],
                               lambda k: hT[:, k, c0:c1], KD)
                for cc in range(2):
                    for j, (c0, c1) in enumerate(TOK3):
                        proj_t(u_ga(g, cc) + j, 4 + g, lambda k: ws[:, k, 256 + cc * P:256 + (cc + 1) * P],
                               lambda k: hT[:, k, META + c0:META + c1], KD)
                pe.wait_ge(win_done, 2 * g + 2)
                pe.wait_ge(wp_in[g % 2], 16 * (g // 2 + 1))
                for cc in range(2):
                    for j, (c0, c1) in enumerate(TOK3):
                        proj_t(u_pool(g, cc) + j, 0, lambda k: wp_v[:, g % 2, k, cc * P:(cc + 1) * P],
                               lambda k: dT[:, k, c0:c1], 2)
            for c in range(KD):
                w = 8 + c // 4
                if c % 4 == 0:
                    pe.wait_ge(w_in_s[w], 16)
                for j, (c0, c1) in enumerate(TOK3):
                    proj_t(u_gb(c) + j, w, lambda k: wslot[w % 2][:, k, (c % 4) * P:(c % 4 + 1) * P],
                           lambda k: hT[:, k, META + c0:META + c1], KD)

            def qk(G, r):
                kind, i, g = AG[G]
                for m, (c0, c1) in enumerate(chunks_of(G)):
                    s = S_AT[G] + r * len(chunks_of(G)) + m
                    if s >= 3:
                        pe.wait_ge(a_sm, s - 2)
                    b = bank[s % 3]
                    if kind == "p":
                        last = mm(b[:, 0:c1 - c0], qT[:, REP * g + r, i * P:(i + 1) * P], kT[:, g, c0:c1],
                                  start=True, stop=True)
                    else:
                        if m == 0:
                            pe.wait_ge(kb_in[i % 3], 64 * (i // 3 + 1))
                            pe.wait_ge(kb_new, i + 1)
                        kt = kTb[:, i % 3, :].rearrange("p (g n) -> p g n", g=KVH)
                        mm(b[:, 0:c1 - c0], repb[:, i, :], sbias[:, c0:c1], start=True, stop=False,
                           skip_group_check=True)
                        for gg in range(KVH):
                            q_b = qsb[:, i % 3, 64 * gg:64 * gg + 64]
                            last = mm(b[64 * gg:64 * gg + 64, 0:c1 - c0], q_b, kt[:, gg, c0:c1],
                                      start=False, stop=True, skip_group_check=True)
                    last.then_inc(a_s, 1)

            def tpv(G):
                kind, i, g = AG[G]
                pe.wait_ge(a_p, U_AT[G + 1])
                ob = bank[5 + G % 2]
                if G >= 2:
                    pe.wait_ge(a_oe, G - 1)
                pb = PB[G % 2]
                if kind == "p":
                    nb = trs_of(G)
                    for j in range(nb + 2):
                        if j < nb:
                            t = T_AT[G] + j
                            if t >= 2:
                                pe.wait_ge(a_te, t - 1)
                            rows = META if j == 0 else P
                            k0 = 0 if j == 0 else META + P * (j - 1)
                            for r in range(REP):
                                last = nc.tensor.transpose(bank[3 + t % 2][0:rows, r * P:(r + 1) * P],
                                                           pb[:, r, k0:k0 + rows], ident)
                            last.then_inc(a_t, 1)
                        if j >= 2:
                            jj = j - 2
                            t = T_AT[G] + jj
                            pe.wait_ge(a_te, t + 1)
                            rows = META if jj == 0 else P
                            last = mm(ob[:, :], vS[0:rows, jj, g * HD:(g + 1) * HD], PT[0:rows, t % 4, :],
                                      start=(jj == 0), stop=(jj == nb - 1))
                    last.then_inc(a_o, 1)
                else:
                    t = T_AT[G]
                    pe.wait_ge(a_te, t - 1)
                    for j in range(4):
                        last = nc.tensor.transpose(bank[3 + t % 2][:, j * P:(j + 1) * P], pb[:, 0, j * P:(j + 1) * P], ident)
                    last.then_inc(a_t, 1)
                    pe.wait_ge(a_te, t)
                    nc.tensor.transpose(bank[3 + (t + 1) % 2][0:32, 0:P], pb[:, 0, 512:SK], ident).then_inc(a_t, 1)
                    pe.wait_ge(a_te, t + 2)
                    v = vb[:, i % 3, :].rearrange("p (j d) -> p j d", j=5)
                    for gg in range(KVH):
                        for j in range(5):
                            rows = P if j < 4 else 32
                            src = PT[0:rows, t % 4, j * P:(j + 1) * P] if j < 4 else PT[0:rows, (t + 1) % 4, 0:P]
                            last = mm(ob[:, 64 * gg:64 * gg + 64], v[0:rows, j, gg * HD:(gg + 1) * HD],
                                      src[:, 64 * gg:64 * gg + 64], start=(j == 0), stop=(j == 4),
                                      skip_group_check=True)
                    last.then_inc(a_o, 1)

            pe.wait_ge(tr_evac, TR_AT[N_NAT])
            pe.wait_ge(pj_evac, u_gb(KD))
            for G in range(-1, len(AG)):
                if G + 1 < len(AG):
                    if G + 1 == 2 * NPT:
                        pe.wait_ge(selected, 8)
                    for r in range(heads_of(G + 1)):
                        qk(G + 1, r)
                if G >= 0:
                    tpv(G)

            pe.wait_ge(w_in_s[10], 16)
            pe.wait_ge(w_in_s[11], 16)
            pe.wait_ge(a_oe, len(AG))
            for c in range(KD):
                for j, (c0, c1) in enumerate(TOK3):
                    u = 3 * c + j
                    if u >= 4:
                        pe.wait_ge(b6_evac, u - 3)
                    for h in range(HEADS):
                        last = mm(bank[u % 4][:, 0:384], wao[h // 4][:, h % 4, c * P:(c + 1) * P], qT[:, h, c0:c1],
                                  start=(h == 0), stop=(h == HEADS - 1))
                    last.then_inc(b6_done, 1)

            def out_proj(t):
                for hf in range(2):
                    u = 2 * t + hf
                    if u >= 2:
                        pe.wait_ge(x2_ready, u - 1)
                    for k in range(KD):
                        last = mm(bank[4 + hf][:, :], mT[:, k, t * P:(t + 1) * P], wout[:, k, hf * 512:(hf + 1) * 512],
                                  start=(k == 0), stop=(k == KD - 1))
                    last.then_inc(o7_done, 1)

            def router(t):
                pe.wait_ge(h2_ready, t + 1)
                for hf in range(2):
                    u = 2 * t + hf
                    if u >= 2:
                        pe.wait_ge(t7_evac, u - 1)
                    for j in range(4):
                        k = 4 * hf + j
                        last = nc.tensor.transpose(bank[6 + hf][:, j * P:(j + 1) * P], h2[:, t % 2, k * P:(k + 1) * P], ident)
                    last.then_inc(t7_done, 1)
                pe.wait_ge(t7_evac, 2 * t + 2)
                if t >= 2:
                    pe.wait_ge(pos_ready, t - 1)
                for k in range(KD):
                    last = mm(bank[t % 2][:, 0:NG + NE], h2T[:, k, :], wrout[:, k, :], start=(k == 0), stop=(k == KD - 1))
                last.then_inc(lg_done, 1)

            def rank(t):
                pe.wait_ge(hot_ready, t + 1)
                mm(bank[t % 2][:, 64:64 + NE], upper, a_bf[:, t, :], start=True, stop=False, skip_group_check=True)
                mm(bank[t % 2][:, 64:64 + NE], onesb, onehots[:, t, :], start=False, stop=True,
                   skip_group_check=True).then_inc(rank_done, 1)

            pe.wait_ge(m_ready, 24)
            pe.wait_ge(wo_in, 16)
            pe.wait_ge(b6_evac, 24)
            for t in range(NT + 2):
                if t < NT:
                    out_proj(t)
                if 1 <= t <= NT:
                    router(t - 1)
                if t >= 2:
                    rank(t - 2)
            pe.wait_ge(pos_ready, NT)
            mm(bank[2][:, 0:NE], onesb, onehots[:, NT, :], start=True, stop=True).then_inc(cnt_done, 1)

            def e_trans(e):
                pe.wait_ge(hg_in[e % 3], 16 * (e // 3 + 1))
                for hf in range(2):
                    u = 2 * e + hf
                    if u >= 2:
                        pe.wait_ge(te_evac, u - 1)
                    for j in range(4):
                        k = 4 * hf + j
                        last = nc.tensor.transpose(bank[4 + hf][:, j * P:(j + 1) * P], hg[:, e % 3, k * P:(k + 1) * P], ident)
                    last.then_inc(te_done, 1)

            def gate_up(e, slot, par):
                for w, o in ((e_gate(slot), 0), (e_up(slot), P)):
                    for k in range(KD):
                        last = mm(bank[6 + par][:, o:o + P], w[:, k, :], hgT[:, par, k, :],
                                  start=(k == 0), stop=(k == KD - 1), skip_group_check=True)
                last.then_inc(gu_done, 1)

            def down(slot, par):
                for hf in range(2):
                    last = mm(bank[2 * par + hf][:, :], actT[:, par, :], e_down(slot)[:, hf * 512:(hf + 1) * 512],
                              start=True, stop=True)
                last.then_inc(dn_done, 1)

            pe.wait_ge(x2_ready, 2 * NT)
            pe.wait_ge(over_ready, 1)
            e_trans(0)
            for e in range(NE):
                pe.wait_ge(ew_in[e % NSLOT], 48 * (e // NSLOT + 1))
                pe.wait_ge(te_evac, 2 * e + 2)
                if e >= 2:
                    pe.wait_ge(act_ready, e - 1)
                gate_up(e, e % NSLOT, e % 2)
                if e + 1 < NE:
                    e_trans(e + 1)
                pe.wait_ge(act_ready, e + 1)
                if e >= 2:
                    pe.wait_ge(y_ready, e - 1)
                down(e % NSLOT, e % 2)

            pe.wait_ge(over_in, 32)
            n_over = pe.value_load(over_row[0:1, 31:32], min_val=0, max_val=MAX_OVER)
            with pe.If(n_over > 0):
                with pe.Fori(0, n_over) as it:
                    pe.wait_ge(ov_h, 16 * it + 16)
                    for hf in range(2):
                        for j in range(4):
                            k = 4 * hf + j
                            last = nc.tensor.transpose(bank[4 + hf][:, j * P:(j + 1) * P], hg[:, 0, k * P:(k + 1) * P], ident)
                    last.then_inc(te_done, 1)
                    pe.wait_ge(te_evac, 2 * NE + 1 + it)
                    pe.wait_ge(ov_w, 48 * it + 48)
                    gate_up(0, 0, 0)
                    pe.wait_ge(act_ready, NE + 1 + it)
                    down(0, 0)

        @block.scalar
        def _(act):
            cp = nc.scalar.copy
            for k in range(KD):
                act.wait_ge(x_in[k], 16)
                if k >= 2:
                    act.wait_ge(sq_used, k - 1)
                nc.scalar.activation(sq[:, k % 2, :], hT[:, k, :], ACT.Square).then_inc(sq_ready, 1)

            act.wait_ge(r_ready, 3)
            nc.scalar.activation(rbc, rbc, ACT.Sqrt).then_inc(root_ready, 1)

            def evac_nat(n):
                kind, tt = NAT[n]
                rows = tcols(tt)[1]
                act.wait_ge(pj_done, n + 1)
                if n >= 3:
                    act.wait_ge(tr_done, TR_AT[n - 2])
                    if n - 3 < N_KV:
                        act.wait_ge(nat_out[n % 3], 16 * ((n - 3) // 3 + 1))
                b = bank[n % 4]
                if kind == "idx":
                    cp(nbuf[0:rows, n % 3, 0:320], b[0:rows, 0:320])
                    nc.scalar.mul(wis[0:rows, tt, :], b[0:rows, 320:324], IDX_SCALE).then_inc(pj_evac, 1)
                elif kind == "kv":
                    cp(nbuf[0:rows, n % 3, 0:256], b[0:rows, 0:256])
                    cp(vS[0:rows, tt, :], b[0:rows, 256:512]).then_inc(pj_evac, 1)
                else:
                    cp(nbuf[:, n % 3, :], b[:, :]).then_inc(pj_evac, 1)

            def evac_tr(n):
                kind, tt = NAT[n]
                c0, rows = tcols(tt)
                v = TR_AT[n]
                act.wait_ge(tr_done, v + 1)
                b = bank[4 + v % 2]
                if kind == "idx" and tt == 0:
                    cp(kiT[:, 0:META], b[:, 0:META]).then_inc(tr_evac, 1)
                elif kind == "idx" and tt < 9:
                    cp(qiT[:, :, c0 - META:c0 - META + P], b[:, 0:256].rearrange("p (j t) -> p j t", j=2))
                    cp(kiT[:, c0:c0 + P], b[:, 256:384]).then_inc(tr_evac, 1)
                elif kind == "idx":
                    act.wait_ge(qib_zero, 1)
                    for u in range(2):
                        dst = qiB[64 * u:64 * u + 64, :, :].rearrange("p h (q x) -> p h q x", x=160)
                        src = b[64 * u:64 * u + 64, :].rearrange("p (h q x) -> p h q x", h=4, x=32)
                        for h in range(IH):
                            last = cp(dst[:, h, :, 16 * u:16 * u + 16], src[:, h, :, 16 * u:16 * u + 16])
                    last.then_inc(tr_evac, 1)
                    act.wait_ge(tr_done, v + 2)
                    act.wait_ge(kic_in, 16)
                    b = bank[4 + (v + 1) % 2]
                    for u in range(2):
                        src = b[64 * u:64 * u + 64, 0:P].rearrange("p (q x) -> p q x", x=32)
                        last = cp(kiC[64 * u:64 * u + 64, :, CACHE:SK], src[:, :, 16 * u:16 * u + 16])
                    last.then_inc(tr_evac, 1)
                elif kind == "kv":
                    src = b[:, 0:256].rearrange("p (g t) -> p g t", g=2)
                    cp(kT[:, :, c0:c0 + rows], src[:, :, 0:rows]).then_inc(tr_evac, 1)
                else:
                    hh = 4 * (kind == "q1")
                    cp(qT[:, hh:hh + 4, c0 - META:c0 - META + P],
                       b[:, :].rearrange("p (j t) -> p j t", j=4)).then_inc(tr_evac, 1)

            def nat_group(lo, hi):
                for n in range(lo, hi + 2):
                    if n < hi:
                        evac_nat(n)
                    if n - 2 >= lo:
                        evac_tr(n - 2)

            act.wait_ge(h_ready, KD)
            act.wait_ge(const_in, 112)
            nat_group(0, N_IDX)
            for s, (i, (c0, c1), h) in enumerate(SCU):
                act.wait_ge(sc_done, s + 1)
                if s >= 3:
                    act.wait_ge(sc_acc, s - 2)
                nc.scalar.activation(rel[:, s % 3, 0:c1 - c0], bank[6 + s % 2][:, 0:c1 - c0], ACT.Relu).then_inc(sc_relu, 1)
            nat_group(N_IDX, N_KV)
            act.wait_ge(list_init, 16)
            nat_group(N_KV, N_NAT)

            act.wait_ge(sc_acc, len(SCU))
            for g in range(4):
                for cc in range(2):
                    zi = 2 * g + cc
                    if zi >= 2:
                        act.wait_ge(win_done, zi - 1)
                        act.wait_ge(pool_out[zi % 2], 32 * (zi // 2))
                    for j, (c0, c1) in enumerate(COL3):
                        u = u_z(g, cc) + j
                        act.wait_ge(pj_done, u + 1)
                        cp(zT[:, zi % 2, c0:c1], bank[u % 4][:, 0:c1 - c0]).then_inc(pj_evac, 1)
                for cc in range(2):
                    c = 2 * g + cc
                    if c >= 2:
                        act.wait_ge(u_done, c - 1)
                    for j, (c0, c1) in enumerate(TOK3):
                        u = u_ga(g, cc) + j
                        act.wait_ge(pj_done, u + 1)
                        nc.scalar.activation(sg[:, c % 2, c0:c1], bank[u % 4][:, 0:384], ACT.Sigmoid).then_inc(pj_evac, 1)
                for cc in range(2):
                    c = 2 * g + cc
                    if c >= 2:
                        act.wait_ge(u_out[c % 2], 16 * (c // 2))
                    for j, (c0, c1) in enumerate(TOK3):
                        u = u_pool(g, cc) + j
                        act.wait_ge(pj_done, u + 1)
                        nc.scalar.mul(ub[:, c % 2, c0:c1], bank[u % 4][:, 0:384], pscale[:, c:c + 1]).then_inc(pj_evac, 1)
            for c in range(KD):
                if c < 2:
                    act.wait_ge(u_done, 7 + c)
                else:
                    act.wait_ge(sb_out[c % 2], 16 * (c // 2))
                for j, (c0, c1) in enumerate(TOK3):
                    u = u_gb(c) + j
                    act.wait_ge(pj_done, u + 1)
                    nc.scalar.activation(sg[:, c % 2, c0:c1], bank[u % 4][:, 0:384], ACT.Sigmoid).then_inc(pj_evac, 1)

            def expo(G, r):
                uu = U_AT[G] + r
                n = chunks_of(G)[-1][1]
                act.wait_ge(a_max, uu + 1)
                p = PB[G % 2][:, r, 0:n]
                nc.scalar.activation(p, p, ACT.Exp, bias=nmx[:, uu % 8:uu % 8 + 1], scale=ATTN_SCALE,
                                     accum_out=rsum[:, uu % 8:uu % 8 + 1]).then_inc(a_exp, 1)

            def tevac(G, j):
                kind = AG[G][0]
                t = T_AT[G] + j
                act.wait_ge(a_t, t + 1)
                if kind == "p":
                    rows = META if j == 0 else P
                    cp(PT[0:rows, t % 4, :], bank[3 + t % 2][0:rows, :]).then_inc(a_te, 1)
                elif j == 0:
                    cp(PT[:, t % 4, :], bank[3 + t % 2][:, :]).then_inc(a_te, 1)
                else:
                    cp(PT[0:32, t % 4, 0:P], bank[3 + t % 2][0:32, 0:P]).then_inc(a_te, 1)

            for s in range(2):
                act.wait_ge(sb_out[s], 64)
                act.wait_ge(u_out[s], 64)
            for G in range(-1, len(AG)):
                nxt = list(range(heads_of(G + 1))) if G + 1 < len(AG) else []
                cur = list(range(trs_of(G))) if G >= 0 else []
                for r in nxt[:3]:
                    expo(G + 1, r)
                for j in cur[:2]:
                    tevac(G, j)
                for r in nxt[3:]:
                    expo(G + 1, r)
                for j in cur[2:]:
                    tevac(G, j)

            def norm2(t):
                act.wait_ge(x2_ready, 2 * t + 2)
                if t >= 2:
                    act.wait_ge(t7_done, 2 * t - 2)
                    act.wait_ge(h2_out[t % 2], 16 * (t // 2))
                nc.scalar.activation(h2[:, t % 2, :], x2[:, t, :], ACT.Square, scale=1.0 / 32.0,
                                     accum_out=tnrm[:, t, 0:1]).then_inc(ms_ready, 1)

            def h2t(t):
                for hf in range(2):
                    act.wait_ge(t7_done, 2 * t + hf + 1)
                    if t >= 1:
                        act.wait_ge(lg_done, t)
                    cp(h2T[:, 4 * hf:4 * hf + 4, :], bank[6 + hf][:, :].rearrange("p (k t) -> p k t", k=4)).then_inc(t7_evac, 1)

            def route_exp(t):
                act.wait_ge(gexp_in, t + 1)
                nc.scalar.activation(r_gexp, r_lg[:, 0:NG], ACT.Exp, bias=r_ngm, accum_out=r_gs).then_inc(gexp_done, 1)
                act.wait_ge(eexp_in, t + 1)
                nc.scalar.activation(r_ex, r_dv, ACT.Exp).then_inc(eexp_done, 1)

            act.wait_ge(b6_evac, 24)
            act.wait_ge(m_ready, 24)
            for t in range(NT + 1):
                if t < NT:
                    norm2(t)
                if t >= 1:
                    h2t(t - 1)
                    route_exp(t - 1)

            def silu_e(par):
                nc.scalar.activation(silu[:, par, :], bank[6 + par][:, 0:P], ACT.Silu).then_inc(silu_done, 1)

            act.wait_ge(o7_done, 2 * NT)
            for e in range(NE):
                if e < NE:
                    for hf in range(2):
                        act.wait_ge(te_done, 2 * e + hf + 1)
                        if e >= 2:
                            act.wait_ge(gu_done, e - 1)
                        cp(hgT[:, e % 2, 4 * hf:4 * hf + 4, :],
                           bank[4 + hf][:, :].rearrange("p (k t) -> p k t", k=4)).then_inc(te_evac, 1)
                    act.wait_ge(gu_done, e + 1)
                    if e >= 2:
                        act.wait_ge(act_ready, e - 1)
                    silu_e(e % 2)
            act.wait_ge(over_in, 32)
            n_over = act.value_load(over_row[0:1, 31:32], min_val=0, max_val=MAX_OVER)
            with act.If(n_over > 0):
                with act.Fori(0, n_over) as it:
                    act.wait_ge(te_done, 2 * NE + 1 + it)
                    for hf in range(2):
                        last = cp(hgT[:, 0, 4 * hf:4 * hf + 4, :], bank[4 + hf][:, :].rearrange("p (k t) -> p k t", k=4))
                    last.then_inc(te_evac, 1)
                    act.wait_ge(gu_done, NE + 1 + it)
                    silu_e(0)
            for t in range(NT):
                act.wait_ge(y1_done, t + 1)
                nc.scalar.activation(ya[:, t % 2, :], x2[:, t, :], ACT.Square, scale=1.0 / 32.0,
                                     accum_out=fnrm[:, t, 0:1]).then_inc(fms_ready, 1)

        @block.vector
        def _(dve):
            tt = nc.vector.tensor_tensor
            ts = nc.vector.tensor_scalar
            stt = nc.vector.scalar_tensor_tensor
            dve_n = [0]

            def link(ins):
                dve_n[0] += 1
                ins.then_inc(dve_c, 1)
                dve.wait_ge(dve_c, dve_n[0])

            nc.vector.memset(ones_f, 1.0 / D).then_inc(ones_ready, 1)
            dve.wait_ge(const_in, 112)
            dve.wait_ge(sq_used, KD)
            for j, (c0, c1) in enumerate(COL3):
                ts(rbc[:, c0:c1], bank[j][:, 0:c1 - c0], EPS, None, ALU.add).then_inc(r_ready, 1)
            dve.wait_ge(root_ready, 1)
            link(nc.vector.reciprocal(rbc, rbc))
            for k in range(KD):
                stt(out=hT[:, k, :], in0=hT[:, k, :], scalar=gmix[:, k:k + 1], in1=rbc,
                    op0=ALU.mult, op1=ALU.mult).then_inc(h_ready, 1)
            nc.vector.memset(qiB[:, :, :], 0.0).then_inc(qib_zero, 1)
            link(nc.vector.memset(sc_s[:, SK:SK + 4], 3.0e38))
            for s, (i, (c0, c1), h) in enumerate(SCU):
                dst = (sc[i] if i < 8 else sc_s)[:, c0:c1]
                w = wis[:, i + 1, h:h + 1]
                dve.wait_ge(sc_relu, s + 1)
                if h == 0:
                    ts(dst, rel[:, s % 3, 0:c1 - c0], w, None, ALU.mult).then_inc(sc_acc, 1)
                else:
                    dve.wait_ge(sc_acc, s)
                    stt(out=dst, in0=rel[:, s % 3, 0:c1 - c0], scalar=w, in1=dst,
                        op0=ALU.mult, op1=ALU.add).then_inc(sc_acc, 1)
            dve.wait_ge(sc_acc, len(SCU))
            for i in range(1, NPT):
                link(nc.vector.memset(sc[i][0:64, n_keys[i] - CHUNK:n_keys[i]], MASKED))

            def rounds(tiles, n):
                base = dve_n[0]
                step = 2 * len(tiles)
                with dve.Fori(0, n) as r:
                    for q, x in enumerate(tiles):
                        nc.vector.max(m8[:, q, :], x).then_inc(dve_c, 1)
                    dve.wait_ge(dve_c, step * r + (base + len(tiles)))
                    nc.vector.memset(vjunk, 0.0)
                    for q, x in enumerate(tiles):
                        nc.vector.match_replace(x, m8[:, q, :], x, TAKEN).then_inc(dve_c, 1)
                    dve.wait_ge(dve_c, step * r + (base + step))
                dve_n[0] += step * n

            def bias_of(i):
                if i == 8:
                    ts(sbias[:, :], sc_s[:, 0:SK], BETWEEN, NEG_BIAS, ALU.is_gt, ALU.mult).then_inc(selected, 1)
                    return
                link(ts(sc[i], sc[i], BETWEEN, NEG_BIAS, ALU.is_gt, ALU.mult))
                nc.vector.memset(sc[i][0:64, n_keys[i] - CHUNK:n_keys[i]], NEG_BIAS).then_inc(selected, 1)

            link(nc.vector.memset(sc[0], 0.0))
            nc.vector.memset(sc[0][0:64, n_keys[0] - CHUNK:n_keys[0]], NEG_BIAS).then_inc(selected, 1)
            for i in (1, 3, 5):
                rounds([sc[i], sc[i + 1]], TOPK_P // 8)
                bias_of(i)
                bias_of(i + 1)
            n_s = (TOPK_S + 4) // 8
            rounds([sc_s, sc[7]], n_s)
            rounds([sc[7]], TOPK_P // 8 - n_s)
            bias_of(8)
            bias_of(7)

            def ttr(G, r):
                kind, i, g = AG[G]
                uu = U_AT[G] + r
                ch = chunks_of(G)
                if G >= 2:
                    dve.wait_ge(a_t, T_AT[G - 1])
                for m, (c0, c1) in enumerate(ch):
                    s = S_AT[G] + r * len(ch) + m
                    dve.wait_ge(a_s, s + 1)
                    add = sc[i][:, c0:c1] if kind == "p" else zero[:, 0:c1 - c0]
                    dst = mx3[:, uu % 8, m:m + 1]
                    nc.vector.tensor_tensor_reduce(out=PB[G % 2][:, r, c0:c1], in0=bank[s % 3][:, 0:c1 - c0], in1=add,
                                                   scale=1.0, scalar=MASKED, op0=ALU.add, op1=ALU.max,
                                                   accum_out=dst).then_inc(a_sm, 1)
                dve.wait_ge(a_sm, s + 1)
                if len(ch) > 1:
                    link(nc.vector.tensor_reduce(mx1[:, uu % 8:uu % 8 + 1], mx3[:, uu % 8, 0:len(ch)], AX.X, ALU.max))
                    src = mx1[:, uu % 8:uu % 8 + 1]
                else:
                    src = mx3[:, uu % 8, 0:1]
                ts(nmx[:, uu % 8:uu % 8 + 1], src, -ATTN_SCALE, None, ALU.mult).then_inc(a_max, 1)

            def recip(uu):
                dve.wait_ge(a_exp, uu + 1)
                nc.vector.reciprocal(rinv[:, uu % 8:uu % 8 + 1], rsum[:, uu % 8:uu % 8 + 1]).then_inc(a_ri, 1)

            def oevac(G):
                kind, i, g = AG[G]
                dve.wait_ge(a_o, G + 1)
                ob = bank[5 + G % 2]
                if kind == "p":
                    nc.vector.tensor_copy(qT[:, REP * g:REP * g + REP, i * P:(i + 1) * P],
                                          ob[:, :].rearrange("p (r t) -> p r t", r=REP)).then_inc(a_oe, 1)
                else:
                    nc.vector.tensor_copy(qT[:, :, SEQ + 16 * i:SEQ + 16 * i + 16],
                                          ob[:, 0:P].rearrange("p (r t) -> p r t", r=HEADS)).then_inc(a_oe, 1)

            dve.wait_ge(pj_done, u_gb(KD))
            nc.vector.memset(zero, 0.0).then_inc(zero_ready, 1)
            dve.wait_ge(zero_ready, 1)
            dve.wait_ge(selected, NT)
            for s in range(2):
                dve.wait_ge(sb_out[s], 64)
                dve.wait_ge(pool_out[s], 128)
            for G in range(-1, len(AG)):
                if G + 1 < len(AG):
                    nh = heads_of(G + 1)
                    for r in range(nh + 1):
                        if r < nh:
                            ttr(G + 1, r)
                        if r >= 1:
                            recip(U_AT[G + 1] + r - 1)
                if G >= 0:
                    oevac(G)

            for c in range(KD):
                dve.wait_ge(sbi_in[c % 2], 16 * (c // 2 + 1))
                dve.wait_ge(mu_in[c], 16)
                for j, (c0, c1) in enumerate(TOK3):
                    u = 3 * c + j
                    dve.wait_ge(b6_done, u + 1)
                    if u >= 3:
                        dve.wait_ge(m_ready, u - 2)
                    tt(mtmp[:, u % 3, :], bank[u % 4][:, 0:384], sB[:, c % 2, c0:c1], ALU.mult).then_inc(b6_evac, 1)
                    dve.wait_ge(b6_evac, u + 1)
                    tt(mT[:, c, c0:c1], mT[:, c, c0:c1], mtmp[:, u % 3, :], ALU.add).then_inc(m_ready, 1)

            def resid(t):
                dve.wait_ge(x2_in[t], 16)
                for hf in range(2):
                    dve.wait_ge(o7_done, 2 * t + hf + 1)
                    part = x2[:, t, hf * 512:(hf + 1) * 512]
                    tt(part, bank[4 + hf][:, :], part, ALU.add).then_inc(x2_ready, 1)

            def h2_of(t):
                dve.wait_ge(rstd_ready, t + 1)
                stt(out=h2[:, t % 2, :], in0=x2[:, t, :], scalar=tnrm[:, t, 1:2], in1=gffn,
                    op0=ALU.mult, op1=ALU.mult).then_inc(h2_ready, 1)

            def route(t):
                lg = bank[t % 2]
                dve.wait_ge(lg_done, t + 1)
                tt(r_lg[:, 0:NG], lg[:, 0:NG], rbias[:, 0:NG], ALU.add)
                link(tt(r_lg[:, 8:8 + NE], lg[:, NG:NG + NE], rbias[:, NG:NG + NE], ALU.add))
                link(nc.vector.max(r_m8g, r_lg[:, 0:8]))
                ts(r_ngm, r_m8g[:, 0:1], -1.0, None, ALU.mult).then_inc(gexp_in, 1)
                link(nc.vector.max_index(r_i8g, r_m8g, r_lg[:, 0:8]))
                link(nc.vector.tensor_copy(r_gsel, r_i8g[:, 0:1]))
                link(ts(r_mk, iota4, r_gsel, None, ALU.is_equal))
                link(ts(r_mk2, r_mk, 1.0, 3.0e38, ALU.subtract, ALU.mult))
                link(tt(r_em, r_lg[:, 8:8 + NE].rearrange("p (a b) -> p a b", a=NG),
                        r_mk2.unsqueeze(2).to_broadcast([P, NG, EPG]), ALU.add))
                link(nc.vector.max(r_m8e, r_emf))
                link(nc.vector.max_index(r_i8e, r_m8e, r_emf))
                tt(r_dv, r_m8e[:, 1:2], r_m8e[:, 0:1], ALU.subtract).then_inc(eexp_in, 1)
                link(nc.vector.tensor_copy(r_if[:, t, :], r_i8e[:, 0:2]))
                ts(r_oh[:, t, 0:NE], iota32, r_if[:, t, 0:1], None, ALU.is_equal)
                link(ts(r_oh[:, t, NE:2 * NE], iota32, r_if[:, t, 1:2], None, ALU.is_equal))
                link(tt(a_bf[:, t, :], r_oh[:, t, 0:NE], r_oh[:, t, NE:2 * NE], ALU.add))
                tt(onehots[:, t + 1, :], onehots[:, t, :], a_bf[:, t, :], ALU.add).then_inc(hot_ready, 1)
                dve.wait_ge(gexp_done, t + 1)
                dve.wait_ge(eexp_done, t + 1)
                link(ts(r_den, r_ex, 1.0, r_gs, ALU.add, ALU.mult))
                link(nc.vector.reciprocal(wts[:, t, 0:1], r_den))
                link(tt(wts[:, t, 1:2], wts[:, t, 0:1], r_ex, ALU.mult))

            def place(t):
                dve.wait_ge(rank_done, t + 1)
                link(nc.vector.tensor_copy(r_rb, bank[t % 2][:, 64:64 + NE]))
                for q in range(2):
                    link(nc.vector.tensor_tensor_reduce(out=r_junk[:, q, :], in0=r_oh[:, t, q * NE:(q + 1) * NE],
                                                        in1=r_rb, scale=1.0, scalar=0.0, op0=ALU.mult, op1=ALU.add,
                                                        accum_out=r_rank[:, t, q:q + 1]))
                link(stt(out=r_pos, in0=r_if[:, t, :], scalar=float(TOK), in1=r_rank[:, t, :], op0=ALU.mult, op1=ALU.add))
                nc.vector.tensor_copy(posi[:, t, :], r_pos).then_inc(pos_ready, 1)
                dve.wait_ge(pos_ready, t + 1)

            dve.wait_ge(g2_in, 16)
            dve.wait_ge(m_ready, 3 * KD)
            link(nc.vector.memset(r_lg[:, 4:8], MASKED))
            link(nc.vector.memset(onehots[:, 0, :], 0.0))
            for t in range(NT + 2):
                if t < NT:
                    resid(t)
                    h2_of(t)
                if 1 <= t <= NT:
                    route(t - 1)
                if t >= 2:
                    place(t - 2)
            dve.wait_ge(cnt_done, 1)
            for s in range(2):
                dve.wait_ge(h2_out[s], 16 * ((NT - s + 1) // 2))
            link(nc.vector.memset(f_one, 1.0))
            link(nc.vector.tensor_copy(r_rb, bank[2][:, 0:NE]))
            link(tt(f_flag, r_rb.unsqueeze(2).to_broadcast([P, NE, OVER_J]),
                    overthr.unsqueeze(1).to_broadcast([P, NE, OVER_J]), ALU.is_gt))
            link(nc.vector.tensor_tensor_scan(f_cum, f_one, f_flag.rearrange("p a b -> p (a b)"), 0.0, ALU.mult, ALU.add))
            link(ts(f_junk, f_cum, siota, 0.0, ALU.is_le, ALU.add, accum_out=f_id))
            link(nc.vector.tensor_copy(over_i[:, 0:1], f_id))
            nc.vector.tensor_copy(over_i[:, 1:2], f_cum[:, NE * OVER_J - 1:NE * OVER_J]).then_inc(over_ready, 1)

            link(nc.vector.memset(f_ob[:, 0:1], 0.0))
            link(nc.vector.tensor_copy(f_ob[:, 1:NE], f_cum.rearrange("p (e j) -> p e j", e=NE)[:, 0:NE - 1, OVER_J - 1]))
            link(stt(out=f_ob, in0=f_ob, scalar=float(P), in1=base32, op0=ALU.mult, op1=ALU.add))
            for t in range(NT):
                for q in range(2):
                    link(nc.vector.tensor_tensor_reduce(out=r_junk[:, q, :], in0=r_oh[:, t, q * NE:(q + 1) * NE],
                                                        in1=f_ob, scale=1.0, scalar=0.0, op0=ALU.mult, op1=ALU.add,
                                                        accum_out=r_sel[:, t, q:q + 1]))
            link(stt(out=r_y1, in0=r_rank, scalar=float(P), in1=r_sel, op0=ALU.is_ge, op1=ALU.mult))
            link(stt(out=r_y2, in0=r_if, scalar=float(P), in1=r_rank, op0=ALU.mult, op1=ALU.add))
            link(tt(r_y1, r_y1, r_y2, ALU.add))
            nc.vector.tensor_copy(ypos[:, :, :], r_y1).then_inc(ypos_ready, 1)

            def act_of(par):
                tt(actT[:, par, :], silu[:, par, :], bank[6 + par][:, P:2 * P], ALU.mult).then_inc(act_ready, 1)

            for e in range(NE + 1):
                if e >= 1:
                    y = e - 1
                    dve.wait_ge(dn_done, y + 1)
                    if y >= 3:
                        dve.wait_ge(y_out[y % 3], 16 * (y // 3))
                    nc.vector.tensor_copy(ysb[:, y % 3, 0:512], bank[2 * (y % 2)][:, :])
                    nc.vector.tensor_copy(ysb[:, y % 3, 512:1024], bank[2 * (y % 2) + 1][:, :]).then_inc(y_ready, 1)
                if e < NE:
                    dve.wait_ge(silu_done, e + 1)
                    if e >= 2:
                        dve.wait_ge(dn_done, e - 1)
                    act_of(e % 2)
            dve.wait_ge(over_in, 32)
            for s in range(3):
                dve.wait_ge(y_out[s], 16 * ((NE - s + 2) // 3))
            n_over = dve.value_load(over_row[0:1, 31:32], min_val=0, max_val=MAX_OVER)
            with dve.If(n_over > 0):
                with dve.Fori(0, n_over) as it:
                    dve.wait_ge(silu_done, NE + 1 + it)
                    act_of(0)
                    dve.wait_ge(dn_done, NE + 1 + it)
                    nc.vector.tensor_copy(ysb[:, 0, 0:512], bank[0][:, :])
                    nc.vector.tensor_copy(ysb[:, 0, 512:1024], bank[1][:, :]).then_inc(y_ready, 1)

            dve.wait_ge(gfin_in, 16)

            def combine(t):
                dve.wait_ge(ya_in[t % 2], 16 * (t // 2 + 1))
                link(stt(out=x2[:, t, :], in0=ya[:, t % 2, :], scalar=wts[:, t, 0:1], in1=x2[:, t, :],
                         op0=ALU.mult, op1=ALU.add))
                dve.wait_ge(yb_in[t % 2], 16 * (t // 2 + 1))
                stt(out=x2[:, t, :], in0=yb[:, t % 2, :], scalar=wts[:, t, 1:2], in1=x2[:, t, :],
                    op0=ALU.mult, op1=ALU.add).then_inc(y1_done, 1)

            def final(t):
                dve.wait_ge(frstd_ready, t + 1)
                stt(out=x2[:, t, :], in0=x2[:, t, :], scalar=fnrm[:, t, 1:2], in1=gfin,
                    op0=ALU.mult, op1=ALU.mult).then_inc(fin_ready, 1)

            for t in range(NT + 1):
                if t < NT:
                    combine(t)
                if t >= 1:
                    final(t - 1)

        @block.gpsimd
        def _(pool):
            tt = nc.gpsimd.tensor_tensor
            pool_n = [0]

            def link(ins):
                pool_n[0] += 1
                ins.then_inc(pool_c, 1)
                pool.wait_ge(pool_c, pool_n[0])

            link(nc.gpsimd.memset(mhalf, -0.5))
            link(nc.gpsimd.memset(zero_i, 0))
            pool.dma_start(list_d.rearrange("(p n) o -> p (n o)", p=P), zero_i).then_inc(list_init, 16)

            def rope(n):
                kind, ti = NAT[n]
                rows = tcols(ti)[1]
                nh, hd, half, o = {"idx": (5, 64, 8, 32), "kv": (2, 128, 16, 0)}.get(kind, (4, 128, 16, 0))
                x = nbuf[0:rows, n % 3, 0:nh * hd].rearrange("p (h d) -> p h d", h=nh)
                x1, x2_ = x[:, :, 0:half], x[:, :, half:2 * half]
                cos = ropec[0:rows, ti, o:o + half].unsqueeze(1).to_broadcast([rows, nh, half])
                sin = ropec[0:rows, ti, o + half:o + 2 * half].unsqueeze(1).to_broadcast([rows, nh, half])
                t4 = [rope_t[0:rows, n % 2, q, 0:nh * half].rearrange("p (h d) -> p h d", h=nh) for q in range(4)]
                pool.wait_ge(pj_evac, n + 1)
                tt(t4[0], x1, cos, ALU.mult)
                tt(t4[1], x2_, sin, ALU.mult)
                tt(t4[2], x2_, cos, ALU.mult)
                link(tt(t4[3], x1, sin, ALU.mult))
                tt(x1, t4[0], t4[1], ALU.subtract)
                last = tt(x2_, t4[2], t4[3], ALU.add)
                if kind == "idx":
                    link(last)
                    last = nc.gpsimd.tensor_copy(nbuf[0:rows, n % 3, 320:384], nbuf[0:rows, n % 3, 256:320])
                    if ti == 9:
                        src = nbuf[:, n % 3, 0:256].rearrange("p (h d) -> p h d", h=IH)
                        for u in range(2):
                            last = nc.gpsimd.tensor_copy(idxd[:, :, u, :], src)
                last.then_inc(rope_done, 1)

            pool.wait_ge(const_in, 112)
            for n in range(N_NAT):
                rope(n)
            pool.wait_ge(tr_done, TR_AT[N_NAT])
            for g in range(2):
                pool.dma_start(wpool[:, g, :, :], a["w_pool"][g].rearrange("(k p) d -> p k d", p=P)).then_inc(wp_in[g], 16)

            def windows(g, cc):
                zi = 2 * g + cc
                q = zi % 2
                pool.wait_ge(pj_evac, u_z(g, cc) + 3)
                pool.wait_ge(st_in[q], 16 * (zi // 2 + 1))
                if cc == 0 and g >= 1:
                    pool.wait_ge(pj_done, u_pool(g - 1, 1) + 3)
                z, z_s = zT[:, q, :], zs[:, q, :, :]
                link(nc.gpsimd.tensor_copy(z_s[:, :, 15:31], z[:, SAMPLE0:COLS].rearrange("p (b s) -> p b s", b=DEC_B)))
                cur, cur_s = z, z_s
                for lv in range(g + 1):
                    sh = 1 << lv
                    lo = 2 * sh - 1
                    nxt, nxt_s = ((wa, za), (wb, zb))[lv % 2]
                    tt(nxt[:, lo:SAMPLE0], cur[:, lo:SAMPLE0], cur[:, lo - sh:SAMPLE0 - sh], ALU.add)
                    link(tt(nxt_s[:, :, lo:31], cur_s[:, :, lo:31], cur_s[:, :, lo - sh:31 - sh], ALU.add))
                    cur, cur_s = nxt, nxt_s
                inv = 1.0 / (2 << g)
                dst_s = dT[:, cc, SEQ:TOK].rearrange("p (b s) -> p b s", b=DEC_B)
                nc.gpsimd.tensor_scalar(cur[:, META:SAMPLE0], cur[:, META:SAMPLE0], inv, None, ALU.mult)
                link(nc.gpsimd.tensor_scalar(cur_s[:, :, 15:31], cur_s[:, :, 15:31], inv, None, ALU.mult))
                tt(dT[:, cc, 0:SEQ], cur[:, META:SAMPLE0], z[:, META:SAMPLE0], ALU.subtract)
                tt(dst_s, cur_s[:, :, 15:31], z_s[:, :, 15:31], ALU.subtract).then_inc(win_done, 1)
                pool.wait_ge(win_done, zi + 1)

            for g in range(4):
                windows(g, 0)
                windows(g, 1)
                for cc in range(2):
                    c = 2 * g + cc
                    pool.wait_ge(pj_evac, u_pool(g, cc) + 3)
                    tt(ub[:, c % 2, :], ub[:, c % 2, :], sg[:, c % 2, :], ALU.mult).then_inc(u_done, 1)
                if g < 2:
                    pool.dma_start(wpool[:, g, :, :], a["w_pool"][g + 2].rearrange("(k p) d -> p k d", p=P)).then_inc(wp_in[g], 16)

            def new_keys(b):
                kt = kTb[:, b % 3, :].rearrange("p (g n) -> p g n", g=KVH)
                if b >= 3:
                    pool.wait_ge(a_o, 2 * NPT + b - 2)
                else:
                    pool.wait_ge(pj_done, u_gb(KD))
                    pool.wait_ge(tr_evac, TR_AT[N_NAT])
                nc.gpsimd.tensor_copy(qsb[:, b % 3, :].rearrange("p (h t) -> p h t", h=HEADS),
                                      qT[:, :, SEQ + 16 * b:SEQ + 16 * b + 16])
                nc.gpsimd.tensor_copy(kt[:, :, CACHE:SK],
                                      kT[:, :, SAMPLE0 + 16 * b:SAMPLE0 + 16 * b + 16]).then_inc(kb_new, 1)

            for b in range(3):
                new_keys(b)
            for G in range(len(AG)):
                for r in range(heads_of(G)):
                    uu = U_AT[G] + r
                    p = PB[G % 2][:, r, 0:chunks_of(G)[-1][1]]
                    pool.wait_ge(a_ri, uu + 1)
                    nc.gpsimd.tensor_scalar(p, p, rinv[:, uu % 8:uu % 8 + 1], None, ALU.mult).then_inc(a_p, 1)
                b = G - 2 * NPT + 2
                if 3 <= b < DEC_B:
                    new_keys(b)

            def rstd(nrm, t):
                link(nc.gpsimd.tensor_scalar(nrm[:, t, 1:2], nrm[:, t, 0:1], EPS, None, ALU.add))
                return tt(nrm[:, t, 1:2], nrm[:, t, 1:2], mhalf, ALU.pow)

            for t in range(NT + 2):
                if t < NT:
                    pool.wait_ge(ms_ready, t + 1)
                    rstd(tnrm, t).then_inc(rstd_ready, 1)
                if t < 2:
                    continue
                t -= 2
                if t == 0:
                    pool.wait_ge(list_init, 16)
                pool.wait_ge(pos_ready, t + 1)
                for q in range(2):
                    pool.indirect_dma_start(out=list_d, out_offset=bass.IndirectOffsetOnAxis(ap=posi[:, t, q:q + 1], axis=0),
                                            in_=tokid[:, t:t + 1], in_offset=None).then_inc(scattered, 16)

            def gather(dst, src, idx, s):
                pool.indirect_dma_start(out=dst, out_offset=None, in_=src,
                                        in_offset=bass.IndirectOffsetOnAxis(ap=idx, axis=0)).then_inc(s, 16)

            pool.wait_ge(lidx_in, 16)
            pool.wait_ge(o7_done, 2 * NT)
            for s in range(2):
                pool.wait_ge(h2_out[s], 16 * ((NT - s + 1) // 2))
            for e in range(NE):
                if e >= 3:
                    pool.wait_ge(te_done, 2 * (e - 2))
                gather(hg[:, e % 3, :], h2_d, lidx[:, e:e + 1], hg_in[e % 3])
            pool.wait_ge(over_in, 32)
            n_over = pool.value_load(over_row[0:1, 31:32], min_val=0, max_val=MAX_OVER)
            with pool.If(n_over > 0):
                pool.wait_ge(dn_done, NE)
                with pool.Fori(0, n_over) as it:
                    code = pool.value_load(over_row[0:1, bass.ds(it, 1)], min_val=0, max_val=NE * OVER_J - 1)
                    ex = pool.snap(code // OVER_J, min_val=0, max_val=NE - 1)
                    row = pool.snap((code // OVER_J) * (TOK - P * OVER_J) + code * P + P, min_val=0, max_val=NE * TOK - P)
                    for dst, src in ((e_gate(0), a["wg"]), (e_up(0), a["wu"])):
                        pool.dma_start(dst, src[bass.ds(ex, 1), :, :].rearrange("o (k p) f -> p (o k) f", p=P)).then_inc(ov_w, 16)
                    pool.dma_start(e_down(0), a["wd"][bass.ds(ex, 1), :, :].rearrange("o p f -> p (o f)")).then_inc(ov_w, 16)
                    pool.dma_start(lidx_o[:, :], list_d[bass.ds(row, P), :]).then_inc(ov_l, 16)
                    pool.wait_ge(ov_l, 16 * it + 16)
                    tt(pjunk, mhalf, mhalf, ALU.add)
                    gather(hg[:, 0, :], h2_d, lidx_o[:, 0:1], ov_h)
                    pool.wait_ge(y_ready, NE + 1 + it)
                    pool.dma_start(y_d[bass.ds(pool.snap(it * P + NE * P, min_val=NE * P, max_val=(NE + MAX_OVER - 1) * P), P), :], ysb[:, 0, :]).then_inc(ov_y, 16)
                    pool.wait_ge(ov_y, 16 * it + 16)
            for s in range(3):
                pool.wait_ge(y_out[s], 16 * ((NE - s + 2) // 3))
            pool.wait_ge(ypos_ready, 1)
            for t in range(NT + 2):
                if t >= 2:
                    pool.wait_ge(fms_ready, t - 1)
                    rstd(fnrm, t - 2).then_inc(frstd_ready, 1)
                if t < NT:
                    gather(ya[:, t % 2, :], y_d, ypos[:, t, 0:1], ya_in[t % 2])
                    gather(yb[:, t % 2, :], y_d, ypos[:, t, 1:2], yb_in[t % 2])


def _constants():
    pos = [np.arange(META)] + [META + P * i + np.arange(P) for i in range(NPT)]
    pos += [CACHE + np.tile(np.arange(DEC_S), DEC_B)]
    c = np.zeros((P, K_END), np.float32)
    c[:, K_ID:K_ID + P] = np.eye(P)
    for t, p in enumerate(pos):
        col = 0
        for rot in (HD // 4, ID // 4):
            half = rot // 2
            inv = np.exp(np.float32(-math.log(500000.0)) * np.arange(half, dtype=np.float32) * np.float32(2.0 / rot))
            ang = p.astype(np.float32)[:, None] * inv.astype(np.float32)[None, :]
            at = K_ROPE + 48 * t + col
            c[:len(p), at:at + half] = np.cos(ang)
            c[:len(p), at + half:at + 2 * half] = np.sin(ang)
            col += 2 * half
    c[:, K_I32:K_I32 + NE] = np.arange(NE)
    c[:, K_BASE:K_BASE + NE] = P * (NE - 1 - np.arange(NE))
    c[:, K_I4:K_I4 + NG] = np.arange(NG)
    c[:, K_SI] = np.arange(P)
    c[:, K_THR:K_THR + OVER_J] = P * (1 + np.arange(OVER_J))
    one = 0x3F80
    b = np.zeros((P, 10 * P), np.uint16)
    for s in range(DEC_B):
        for m in range(P):
            b[16 * s + m % 16, s * P + m] = one
    b[:, 8 * P:9 * P] = np.triu(np.full((P, P), one, np.uint16), 1)
    b[:, 9 * P:] = one
    tok = (np.arange(NT)[None, :] * P + np.arange(P)[:, None]).astype(np.int32)
    return c, b, tok


def kernel(**inp):
    import concourse.bacc as bacc
    from concourse.bass_utils import run_bass_kernel_spmd

    f = {k: np.asarray(v) for k, v in inp.items()}
    c, b, tok = _constants()
    xp, xs = f["x_prompt"][0], f["x_sample"].reshape(DEC_B * DEC_S, D)
    arrays = {
        "xT": np.concatenate([f["meta_tokens"], xp, xs], axis=0).T,
        "x": np.concatenate([xp, xs], axis=0),
        "gmix": f["norm_mix_g"][0].reshape(KD, P).T,
        "pscale": f["pool_scale"][0].reshape(KD, P).T,
        "gffn": np.broadcast_to(f["norm_ffn_g"][0], (P, D)),
        "gfin": np.broadcast_to(f["norm_final_g"], (P, D)),
        "w_in": f["w_in"][0],
        "w_pool": f["w_pool"][0],
        "w_attn_out": f["w_attn_out"][0],
        "w_out": f["w_out"][0],
        "wrout": np.concatenate([f["w_router_group"][0], f["w_router_expert"][0]], axis=1),
        "rbias": np.broadcast_to(np.concatenate([f["b_router_group"][0], f["b_router_expert"][0]]), (P, NG + NE)),
        "wg": f["w_expert_gate"][0], "wu": f["w_expert_up"][0], "wd": f["w_expert_down"][0],
        "ckT": f["cache_k"][0].transpose(0, 2, 3, 1),
        "cv": f["cache_v"][0].reshape(DEC_B, CACHE, KVH * HD),
        "kiC": f["cache_idx_k"][0].transpose(0, 2, 1).reshape(DEC_B // 2, 2 * ID, CACHE),
        "stateT": f["state_pool"][0].transpose(0, 2, 1),
        "consts": c, "cbf": b, "tokid": tok,
    }
    outs = {"o_y": (SEQ, D), "o_ys": (DEC_B * DEC_S, D), "o_k": (META + SEQ, 256), "o_v": (META + SEQ, 256),
            "o_ki": (META + SEQ, ID), "o_poolT": (D, POOL_STATE), "o_ks": (P, 256), "o_vs": (P, 256), "o_kis": (P, ID),
            "o_poolsT": (DEC_B, D, POOL_STATE)}
    nc = bacc.Bacc("TRN2", target_bir_lowering=False, num_devices=1)
    a, feed = {}, {}
    for name, arr in arrays.items():
        arr = np.ascontiguousarray(arr)
        feed[f"in_{name}"] = arr
        a[name] = nc.dram_tensor(f"in_{name}", arr.shape, mybir.dt.from_np(arr.dtype), kind="ExternalInput").ap()
    for name, shape in outs.items():
        a[name] = nc.dram_tensor(f"out_{name}", shape, F32, kind="ExternalOutput").ap()
    build(nc, a)
    r = run_bass_kernel_spmd(nc, [feed], core_ids=[0]).results[0]
    o = {name: r[f"out_{name}"] for name in outs}
    return (o["o_y"].reshape(1, SEQ, D), o["o_ys"].reshape(DEC_B, DEC_S, D),
            o["o_k"].reshape(1, 1, META + SEQ, KVH, HD), o["o_v"].reshape(1, 1, META + SEQ, KVH, HD),
            o["o_ki"].reshape(1, 1, META + SEQ, ID), o["o_poolT"].T.reshape(1, 1, POOL_STATE, D),
            o["o_ks"].reshape(1, DEC_B, DEC_S, KVH, HD), o["o_vs"].reshape(1, DEC_B, DEC_S, KVH, HD),
            o["o_kis"].reshape(1, DEC_B, DEC_S, ID), o["o_poolsT"].transpose(0, 2, 1).reshape(1, DEC_B, POOL_STATE, D))
```

```python
import math
from contextlib import ExitStack

import numpy as np

import concourse.bass as bass
from concourse import mybir

F32 = mybir.dt.float32
F32R = mybir.dt.float32r
BF16 = mybir.dt.bfloat16
I32 = mybir.dt.int32
U32 = mybir.dt.uint32
ALU = mybir.AluOpType
ACT = mybir.ActivationFunctionType
AX = mybir.AxisListType

P = 128
D = 1024
KD = D // P
META = 16
SEQ = 1024
DEC_B, DEC_S = 8, 16
PAST = 512
CHUNK = 64
NPT = SEQ // P
NT = NPT + 1
COLS = META + SEQ + DEC_B * DEC_S
TOK = COLS - META
SAMPLE0 = META + SEQ
EPS = 1e-6
HEADS, KVH, HD, REP = 8, 2, 128, 4
IH, ID = 4, 64
TOPK_P = 256
TOPK_S = (PAST + DEC_S) // 4
CACHE = META + PAST
SK = CACHE + DEC_S
ATTN_SCALE = HD ** -0.5
IDX_SCALE = (IH * ID) ** -0.5
POOL_STATE = 15
C_Z, C_Q, C_KV, C_IDX, C_GA, C_GB = 0, 1024, 2048, 2560, 2884, 3908
IDXW = IH * ID + ID + IH
NE, DE = 32, 128
NG, EPG = 4, 8
MAX_OVER = 2 * TOK // P
OVER_J = TOK // P - 1
MASKED = -3.0e38
TAKEN = -3.4e38
BETWEEN = -3.2e38
NEG_BIAS = -1.0e30

K_ID, K_ROPE, K_I32, K_BASE, K_I4, K_SI, K_THR = 0, 128, 128 + 480, 640, 672, 676, 677
K_END = K_THR + OVER_J


def splits(n, most=512):
    k = -(-n // most)
    w = -(-n // k)
    return [(c, min(c + w, n)) for c in range(0, n, w)]


def build(nc, a):
    ctx = ExitStack()
    with ctx:
        def sb(name, shape, dt=F32):
            return ctx.enter_context(nc.sbuf_tensor(name, shape, dt))

        def sem(name):
            return ctx.enter_context(nc.semaphore(name))

        def sems(name, n):
            return [sem(f"{name}{i}") for i in range(n)]

        RQ = sb("region_q", [P, 9216])
        RK = sb("region_kv", [P, 10240])
        RS = sb("region_s", [P, 1040])
        consts = sb("consts", [P, K_END])
        cbf_raw = sb("cbf", [P, 10 * P], mybir.dt.uint16)
        tokid = sb("tokid", [P, NT], I32)
        nbuf_t = sb("nbuf", [P, 1536])
        small = sb("small", [P, 528])
        small_i = sb("small_i", [P, 2 * NT * 2 + NE + 3], I32)
        sbias = sb("sbias", [P, SK], BF16)
        with ExitStack() as early:
            def sb_early(name, shape, dt):
                return early.enter_context(nc.sbuf_tensor(name, shape, dt))

            h_hi = sb_early("h_hi", [P, KD, COLS], F32R)
            h_lo = sb_early("h_lo", [P, KD, COLS], F32R)
            w_hi_t = sb_early("w_hi", [P, 2 * KD * 256], F32R)
            w_lo_t = sb_early("w_lo", [P, 2 * KD * 256], F32R)
            stage_t = sb_early("w_stage", [P, 4 * 512], F32)
        RH = sb("region_h", [P, 9344])
        RT = sb("region_t", [P, 11392])
        RW = sb("region_w", [P, 8192])

        def view(r, off, *dims):
            n = int(np.prod(dims))
            v = r[:, off:off + n]
            if len(dims) == 2:
                v = v.rearrange("p (a b) -> p a b", a=dims[0])
            if len(dims) == 3:
                v = v.rearrange("p (a b c) -> p a b c", a=dims[0], b=dims[1])
            return v

        sm_at = [0]

        def sm(*dims):
            off = sm_at[0]
            sm_at[0] += int(np.prod(dims))
            assert sm_at[0] <= 528
            return view(small, off, *dims)

        cbf = cbf_raw[:, :].bitcast(BF16)
        ident = consts[:, K_ID:K_ID + P]
        ropec = consts[:, K_ROPE:K_ROPE + 480].rearrange("p (t c) -> p t c", t=10)
        iota32 = consts[:, K_I32:K_I32 + NE]
        base32 = consts[:, K_BASE:K_BASE + NE]
        iota4 = consts[:, K_I4:K_I4 + NG]
        siota = consts[:, K_SI:K_SI + 1]
        overthr = consts[:, K_THR:K_THR + OVER_J]
        repb = cbf[:, 0:8 * P].rearrange("p (b m) -> p b m", b=8)
        upper = cbf[:, 8 * P:9 * P]
        onesb = cbf[:, 9 * P:10 * P]

        gmix = sm(KD)
        pscale = sm(KD)
        wis = sm(10, IH)
        rbias = sm(NG + NE)
        wrout = sm(KD, NG + NE)
        mx3 = sm(8, 3)
        mx1 = sm(8)
        nmx = sm(8)
        rsum = sm(8)
        rinv = sm(8)
        m8 = sm(2, 8)
        tnrm = sm(NT, 2)
        wts = sm(NT, 2)
        fnrm = sm(NT, 2)
        mhalf = sm(1)
        vjunk = sm(1)
        pjunk = sm(1)
        assert sm_at[0] <= 528
        def ints(off, *dims):
            n = int(np.prod(dims))
            v = small_i[:, off:off + n]
            return v if len(dims) == 1 else v.rearrange("p (a b) -> p a b", a=dims[0])

        ypos = ints(0, NT, 2)
        posi = ints(2 * NT, NT, 2)
        lidx = ints(4 * NT, NE)
        over_i = ints(4 * NT + NE, 2)
        lidx_o = ints(4 * NT + NE + 2, 1)
        over_row = sb("over_row", [1, 32], I32)

        xk = view(RK, 0, KD, COLS)
        sq = view(RQ, 0, 2, COLS)
        rbc = view(RQ, 2 * COLS, COLS)
        ones_f = view(RQ, 3 * COLS, P)
        zero_i = RS[:, 0:NE * TOK // P].bitcast(I32)
        rope_t = RS[:, 768:1024].rearrange("p (q c) -> p q c", q=4)

        def w_hi(s, w=256):
            return w_hi_t[:, 2048 * s:2048 * s + KD * w].rearrange("p (k n) -> p k n", k=KD)

        def w_lo(s, w=256):
            return w_lo_t[:, 2048 * s:2048 * s + KD * w].rearrange("p (k n) -> p k n", k=KD)

        def stage(s, w):
            return stage_t[:, 512 * s:512 * s + 2 * w].rearrange("p (k n) -> p k n", k=2)

        qiT = view(RQ, 0, 2, SEQ)
        kiT = view(RQ, 2048, SEQ + META)
        qiB = view(RQ, 3088, IH, 640)
        kiC = view(RQ, 3088 + 2560, 4, SK)
        idxd = view(RQ, 7824, IH, 2, ID)
        rel = view(RS, 0, 2, 384)
        vS = view(RK, 0, 10, 256)
        kT = view(RK, 2560, KVH, COLS)
        n_keys = [META + P * (i + 1) for i in range(NPT)]
        s_off = [4896 + sum(n_keys[:i]) for i in range(NPT)]
        sc = [RK[:, s_off[i]:s_off[i] + n_keys[i]] for i in range(NPT)]
        s_off_s = s_off[-1] + n_keys[-1]
        assert s_off_s + SK + 4 <= 10240
        sc_s = RK[:, s_off_s:s_off_s + SK + 4]
        qT = view(RQ, 0, HEADS, TOK)
        zT = view(RQ, 0, 2, COLS)
        wa = view(RQ, 2336, SAMPLE0)
        dT = view(RQ, 3376, 2, TOK)
        sg = view(RQ, 5680, 2, TOK)
        za, zb = view(RS, 0, DEC_B, 31), view(RS, 248, DEC_B, 31)
        nbuf = nbuf_t[:, :].rearrange("p (a b) -> p a b", a=6)
        nflat = nbuf_t[:, :]
        wpool = nflat[:, 0:1024].rearrange("p (g k d) -> p g k d", g=2, k=2)
        zs = nflat[:, 1024:1520].rearrange("p (a b c) -> p a b c", a=2, b=DEC_B)
        PB = [view(RT, 0, REP, 1040), view(RT, 4160, REP, 1040)]
        PT = view(RT, 8320, 4, 512)
        kTb = view(RH, 0, 3, KVH * SK)
        vb = view(RH, 3 * KVH * SK, 3, 5 * 256)
        zero = RH[:, 7104:7104 + 272]
        qsb = view(RH, 7376, 3, HEADS * DEC_S)
        wao = [view(RW, 0, 4, D), view(RW, 4096, 4, D)]
        mT = view(RH, 0, KD, TOK)
        wout = view(RT, 0, KD, D)
        sB = view(RT, 8192, 2, TOK)
        mtmp = view(RT, 10496, 2, 384)
        x2 = view(RK, 0, NT, D)
        gffn = RK[:, 9216:10240]
        h2 = view(RT, 8192, 2, D)
        h2T = view(RT, 10240, KD, P)
        rt = RS
        eslot = ([RW[:, 0:3072], RW[:, 3072:6144]] + [RQ[:, 3072 * i:3072 * i + 3072] for i in range(3)]
                 + [RH[:, 3072 * i:3072 * i + 3072] for i in range(3)])
        NSLOT = len(eslot)

        def e_gate(s):
            return eslot[s][:, 0:1024].rearrange("p (k f) -> p k f", k=KD)

        def e_up(s):
            return eslot[s][:, 1024:2048].rearrange("p (k f) -> p k f", k=KD)

        def e_down(s):
            return eslot[s][:, 2048:3072]

        hg = view(RT, 0, 3, D)
        hgT = view(RT, 3072, 2, KD, P)
        silu = view(RT, 5120, 2, P)
        actT = view(RT, 5376, 2, P)
        ysb = view(RT, 5632, 3, D)
        ya = view(RT, 8704, 2, D)
        yb = view(RT, 3072, 2, D)
        gfin = RT[:, 1024:2048]

        r_at = [0]

        def rtile(*dims, dt=None):
            n = int(np.prod(dims)) // (2 if dt == BF16 else 1)
            v = rt[:, r_at[0]:r_at[0] + n]
            r_at[0] += n
            assert r_at[0] <= 1040
            if dt is not None:
                v = v.bitcast(dt)
            return v if len(dims) == 1 else v.rearrange("p (a b) -> p a b", a=dims[0])

        r_lg = rtile(40)
        r_m8g = rtile(8)
        r_i8g = rtile(8, dt=U32)
        r_ngm = rtile(1)
        r_gsel = rtile(1)
        r_gexp = rtile(4)
        r_gs = rtile(1)
        r_mk = rtile(4)
        r_mk2 = rtile(4)
        r_em = rtile(NG, EPG)
        r_emf = r_em.rearrange("p a b -> p (a b)")
        r_m8e = rtile(8)
        r_i8e = rtile(8, dt=U32)
        r_dv = rtile(1)
        r_ex = rtile(1)
        r_den = rtile(1)
        r_rb = rtile(NE)
        r_junk = rtile(2, NE)
        r_oh = nflat[:, 0:NT * 2 * NE].rearrange("p (t e) -> p t e", t=NT)
        r_if = rtile(NT, 2)
        r_rank = rtile(NT, 2)
        r_sel = rtile(NT, 2)
        r_y1 = rtile(NT, 2)
        r_y2 = rtile(NT, 2)
        onehots = rtile(NT + 1, NE, dt=BF16)
        a_bf = rtile(NT, NE, dt=BF16)
        r_pos = rtile(2)
        f_flag = view(RT, 8192, NE, OVER_J)
        f_cum = view(RT, 8192 + NE * OVER_J, NE * OVER_J)
        f_one = view(RT, 8192 + 2 * NE * OVER_J, NE * OVER_J)
        f_junk = view(RT, 8192 + 3 * NE * OVER_J, NE * OVER_J)
        f_id = view(RT, 8192 + 4 * NE * OVER_J, 1)
        f_ob = view(RT, 8200 + 4 * NE * OVER_J, NE)

        bank = [ctx.enter_context(nc.psum_tensor(f"bank{i}", [P, 512], F32)) for i in range(8)]

        uA_d = nc.dram_tensor("gated_pool_scratch", (KD, P, TOK), F32, kind="Internal").ap()
        sB_d = nc.dram_tensor("gate_b_scratch", (KD, P, TOK), F32, kind="Internal").ap()
        h2_d = nc.dram_tensor("ffn_input_scratch", (TOK, D), F32, kind="Internal").ap()
        y_d = nc.dram_tensor("expert_rows_scratch", ((NE + MAX_OVER) * P, D), F32, kind="Internal").ap()
        list_d = nc.dram_tensor("expert_lists_scratch", (NE * TOK, 1), I32, kind="Internal").ap()
        over_d = nc.dram_tensor("overflow_table_scratch", (32, 1), I32, kind="Internal").ap()

        COL3 = [(0, 400), (400, 784), (784, COLS)]
        TOK3 = [(0, 384), (384, 768), (768, 1152)]
        PIECES = [("ki", 0, C_IDX + 256, ID + IH), ("qi", 0, C_IDX, 256), ("v", 0, C_KV + 256, 256), ("k", 0, C_KV, 256)]
        for g in range(4):
            PIECES += [("z", g, C_Z + 256 * g, 256), ("ga", g, C_GA + 256 * g, 256)]
        PIECES += [("gb", b, C_GB + 256 * b, 256) for b in range(4)]
        PIECES += [("q", b, C_Q + 256 * b, 256) for b in range(4)]
        NPC = len(PIECES)
        GB0 = 12
        TILES = {"ki": range(10), "qi": range(1, 10), "v": range(10), "k": range(10), "q": range(1, 10)}
        AFTER = {5: 0, 7: 1, 9: 2, 11: 3}
        U = {}
        W_LAST = []
        for n, (kind, b, c0, wd) in enumerate(PIECES):
            for x in (TILES[kind] if kind in TILES else [(cc, j) for cc in range(2) for j in range(3)]):
                U[kind, b, x] = len(U)
            W_LAST.append(len(U))
            if n in AFTER:
                for x in [(cc, j) for cc in range(2) for j in range(3)]:
                    U["pool", AFTER[n], x] = len(U)
        NU = len(U)
        ROPED = [(kind, b, tt) for kind, b, _, _ in PIECES if kind in ("ki", "qi", "k", "q") for tt in TILES[kind]]
        RI = {key: i for i, key in enumerate(ROPED)}
        N_IDX = 19
        N_K = 29
        LAG = 3
        RUNS = [[(kind, b, tt) for kind, b, _, _ in PIECES if kind in kinds for tt in TILES[kind]]
                for kinds in (("ki", "qi", "v"), ("k",), ("q",))]

        def tcols(tt):
            if tt == 0:
                return 0, META
            return META + P * (tt - 1), P

        def out_count(s, r):
            return 16 * len([i for i in range(r) if i % 6 == s and ROPED[i][0] in ("ki", "k")])

        def first_tile(key):
            kind, b, tt = key
            if tt != TILES[kind][0]:
                return None
            return [n for n, pc in enumerate(PIECES) if pc[0:2] == (kind, b)][0]

        SCU = [(i, c, h) for i in range(1, NPT) for c in splits(n_keys[i], 384) for h in range(IH)]
        SCU += [(8, c, h) for c in splits(SK) for h in range(IH)]
        SEL_ORDER = [0, 1, 2, 3, 4, 5, 6, 8, 7]

        AG = [("p", i, g) for i in range(NPT) for g in range(KVH)] + [("s", b, 0) for b in range(DEC_B)]

        def heads_of(G):
            return REP if AG[G][0] == "p" else 1

        def chunks_of(G):
            return splits(n_keys[AG[G][1]]) if AG[G][0] == "p" else splits(SK)

        def trs_of(G):
            return AG[G][1] + 2 if AG[G][0] == "p" else 2

        U_AT = [sum(heads_of(x) for x in range(G)) for G in range(len(AG) + 1)]
        S_AT = [sum(heads_of(x) * len(chunks_of(x)) for x in range(G)) for G in range(len(AG) + 1)]
        T_AT = [sum(trs_of(x) for x in range(G)) for G in range(len(AG) + 1)]

        x_in = sems("x_in", KD)
        const_in = sem("const_in")
        sq_ready = sem("sq_ready")
        sq_used = sem("sq_used")
        r_ready = sem("mean_square_plus_eps")
        root_ready = sem("root_ready")
        rstd_ready = sem("rstd_ready")
        frstd_ready = sem("final_rstd_ready")
        h_ready = sem("h_ready")
        ones_ready = sem("ones_ready")
        stage_in = sems("w_stage_in", 4)
        w_hi_done = sem("w_high_done")
        w_lo_done = sem("w_rest_done")
        h_full = sem("h_full")
        h_high = sem("h_high")
        wao_in = sem("w_attn_out_in")
        wp_in = sems("w_pool_in", 2)
        pj_done = sem("proj_done")
        pj_evac = sem("proj_evacuated")
        tr_done = sem("transposed")
        tr_evac = sem("transposed_evacuated")
        rope_done = sem("rope_done")
        nat_out = sems("nat_out", 6)
        v_out = sem("v_out")
        qib_zero = sem("qib_zero")
        kic_in = sem("kic_in")
        sc_done = sem("score_done")
        sc_relu = sem("score_relu")
        sc_acc = sem("score_accumulated")
        selected = sem("selected")
        dve_c = sem("dve_chain")
        act_c = sem("act_chain")
        pool_c = sem("pool_chain")
        st_in = sems("pool_state_in", 2)
        win_done = sem("windows_done")
        pool_out = sems("pool_rows_out", 2)
        u_done = sem("gated_pool_done")
        u_out = sems("gated_pool_out", 2)
        sb_out = sems("gate_b_out", 2)
        kb_in = sems("cache_in", 3)
        kb_new = sem("cache_new_keys")
        zero_ready = sem("zero_ready")
        a_s = sem("logits_done")
        a_sm = sem("logits_taken")
        a_max = sem("max_ready")
        a_exp = sem("exp_done")
        a_ri = sem("inverse_sum_ready")
        a_p = sem("probs_ready")
        a_t = sem("probs_transposed")
        a_te = sem("probs_transposed_evacuated")
        a_o = sem("head_output_done")
        a_oe = sem("head_output_evacuated")
        mu_in = sems("gated_pool_in", 2)
        sbi_in = sems("gate_b_in", 2)
        wo_in = sem("w_out_in")
        b6_done = sem("attn_out_done")
        b6_evac = sem("attn_out_evacuated")
        m_ready = sem("merged_ready")
        x2_in = sem("x2_in")
        g2_in = sem("gffn_in")
        o7_done = sem("out_proj_done")
        x2_ready = sem("x2_ready")
        ms_ready = sem("mean_square_ready")
        h2_ready = sem("h2_ready")
        h2_out = sems("h2_out", 2)
        t7_done = sem("h2_transposed")
        t7_evac = sem("h2_transposed_evacuated")
        lg_done = sem("router_logits_done")
        gexp_in = sem("group_exp_wanted")
        gexp_done = sem("group_exp_done")
        eexp_in = sem("expert_exp_wanted")
        eexp_done = sem("expert_exp_done")
        hot_ready = sem("onehot_ready")
        rank_done = sem("rank_done")
        pos_ready = sem("positions_ready")
        y_init = sem("overflow_rows_initialised")
        ypos_ready = sem("row_positions_ready")
        list_init = sem("lists_initialised")
        scattered = sem("lists_scattered")
        cnt_done = sem("counts_done")
        over_ready = sem("overflow_table_ready")
        over_out = sem("overflow_table_out")
        over_in = sem("overflow_table_in")
        lidx_in = sem("list_heads_in")
        ew_in = sems("expert_weights_in", NSLOT)
        hg_in = sems("rows_gathered", 3)
        te_done = sem("rows_transposed")
        te_evac = sem("rows_transposed_evacuated")
        gu_done = sem("gate_up_done")
        silu_done = sem("silu_done")
        act_ready = sem("act_ready")
        dn_done = sem("down_done")
        y_ready = sem("y_ready")
        y_out = sems("y_out", 3)
        ov_w = sem("over_weights_in")
        ov_c = sem("over_filler_done")
        ov_l = sem("over_list_in")
        ov_h = sem("over_rows_in")
        ov_y = sem("over_y_out")
        gfin_in = sem("gfin_in")
        ya_in = sems("ya_in", 2)
        yb_in = sems("yb_in", 2)
        y1_done = sem("row_sum_done")
        fms_ready = sem("final_mean_square_ready")
        fin_ready = sem("final_ready")
        fin_out = sem("final_out")

        block = ctx.enter_context(nc.Block())

        w_v = a["w_in"].rearrange("(k p) n -> p k n", p=P)

        @block.sync
        def _(sp):
            for k in range(KD):
                sp.dma_start(xk[:, k, :], a["xT"][k * P:(k + 1) * P, :]).then_inc(x_in[k], 16)
            sp.dma_start(gmix, a["gmix"]).then_inc(const_in, 16)
            sp.dma_start(pscale, a["pscale"]).then_inc(const_in, 16)
            sp.dma_start(consts[:, :], a["consts"]).then_inc(const_in, 16)
            sp.dma_start(cbf_raw[:, :], a["cbf"]).then_inc(const_in, 16)
            sp.dma_start(tokid[:, :], a["tokid"]).then_inc(const_in, 16)
            sp.dma_start(rbias, a["rbias"]).then_inc(const_in, 16)
            sp.dma_start(wrout, a["wrout"].rearrange("(k p) e -> p k e", p=P)).then_inc(const_in, 16)

            def load_piece(n):
                kind, b, c0, wd = PIECES[n]
                for m in range(4):
                    s = 4 * n + m
                    if s >= 4:
                        sp.wait_ge(w_lo_done, s - 3)
                    sp.dma_start(stage(s % 4, wd), w_v[:, 2 * m:2 * m + 2, c0:c0 + wd]).then_inc(stage_in[s % 4], 16)

            load_piece(0)
            sp.dma_start(kiC[:, :, 0:CACHE], a["kiC"].rearrange("q p s -> p q s")).then_inc(kic_in, 16)

            def rows_out(key):
                kind, b, tt = key
                c0, rows = tcols(tt)
                if kind == "v":
                    sp.wait_ge(pj_evac, U[key] + 1)
                    dst = a["o_v"][c0:c0 + rows, :] if tt < 9 else a["o_vs"]
                    sp.dma_start(dst, vS[0:rows, tt, :]).then_inc(v_out, 16)
                    return
                r = RI[key]
                sp.wait_ge(rope_done, r + 1)
                w, o, os = (ID, "o_ki", "o_kis") if kind == "ki" else (256, "o_k", "o_ks")
                dst = a[o][c0:c0 + rows, :] if tt < 9 else a[os]
                sp.dma_start(dst, nbuf[0:rows, r % 6, 0:w]).then_inc(nat_out[r % 6], 16)

            for n, (kind, b, c0, wd) in enumerate(PIECES):
                if n + 1 < NPC:
                    load_piece(n + 1)
                if kind in ("ki", "v", "k"):
                    for tt in TILES[kind]:
                        rows_out((kind, b, tt))

            def cache_in(b):
                if b >= 3:
                    sp.wait_ge(a_o, 2 * NPT + b - 2)
                s = b % 3
                v = vb[:, s, :].rearrange("p (j d) -> p j d", j=5)
                kt = kTb[:, s, :].rearrange("p (g n) -> p g n", g=KVH)
                sp.dma_start(kt[:, :, 0:CACHE], a["ckT"][b].rearrange("g d s -> d g s")).then_inc(kb_in[s], 16)
                sp.dma_start(v[:, 0:4, :], a["cv"][b, 0:512, :].rearrange("(j p) d -> p j d", p=P)).then_inc(kb_in[s], 16)
                sp.dma_start(v[0:16, 4, :], a["cv"][b, 512:CACHE, :]).then_inc(kb_in[s], 16)
                sp.dma_start(v[16:32, 4, :], vS[16 * b:16 * b + 16, 9, :]).then_inc(kb_in[s], 16)

            sp.wait_ge(pj_done, NU)
            w_ao = a["w_attn_out"].rearrange("(k p) n -> p k n", p=P)
            for h in range(2):
                sp.dma_start(wao[h], w_ao[:, 4 * h:4 * h + 4, :]).then_inc(wao_in, 16)
            for b in range(DEC_B):
                cache_in(b)
                if b == 2:
                    sp.wait_ge(zero_ready, 1)
                    sp.dma_start(y_d[NE * P:(NE + MAX_OVER) * P, :].rearrange("(p r) (s c) -> p (r s) c", p=P, c=256),
                                 zero[:, 0:256].unsqueeze(1).to_broadcast([P, MAX_OVER * D // 256, 256])).then_inc(y_init, 16)
            sp.wait_ge(a_oe, len(AG))
            sp.wait_ge(y_init, 16)
            for s in range(2):
                sp.wait_ge(u_out[s], 64)
                sp.wait_ge(sb_out[s], 64)
            for c in range(2):
                sp.dma_start(mT[:, 4 * c:4 * c + 4, :],
                             uA_d[4 * c:4 * c + 4, :, :].rearrange("c p t -> p c t")).then_inc(mu_in[c], 16)
                sp.dma_start(sB[:, c, :], sB_d[c, :, :]).then_inc(sbi_in[c], 16)
            w_o = a["w_out"].rearrange("(k p) n -> p k n", p=P)
            for c in range(2, KD):
                sp.wait_ge(b6_evac, 3 * (c - 1))
                sp.dma_start(sB[:, c % 2, :], sB_d[c, :, :]).then_inc(sbi_in[c % 2], 16)
                if c == 2:
                    sp.dma_start(wout, w_o).then_inc(wo_in, 16)
                    sp.dma_start(x2, a["x"].rearrange("(t p) d -> p t d", p=P)).then_inc(x2_in, 16)
                    sp.dma_start(gffn, a["gffn"]).then_inc(g2_in, 16)

            def load_e(e):
                s = e % NSLOT
                sp.dma_start(e_gate(s), a["wg"][e].rearrange("(k p) f -> p k f", p=P)).then_inc(ew_in[s], 16)
                sp.dma_start(e_up(s), a["wu"][e].rearrange("(k p) f -> p k f", p=P)).then_inc(ew_in[s], 16)
                sp.dma_start(e_down(s), a["wd"][e]).then_inc(ew_in[s], 16)

            sp.wait_ge(b6_done, 24)
            for e in range(5):
                load_e(e)
            for t in range(NT):
                sp.wait_ge(h2_ready, t + 1)
                sp.dma_start(h2_d[t * P:(t + 1) * P, :], h2[:, t % 2, :]).then_inc(h2_out[t % 2], 16)
            sp.wait_ge(o7_done, 2 * NT)
            for e in range(5, NSLOT):
                load_e(e)
            sp.wait_ge(over_ready, 1)
            sp.dma_start(over_d[0:MAX_OVER, :], over_i[0:MAX_OVER, 0:1]).then_inc(over_out, 16)
            sp.dma_start(over_d[31:32, :], over_i[0:1, 1:2]).then_inc(over_out, 16)
            sp.wait_ge(over_out, 32)
            sp.dma_start(over_row[0:1, 0:MAX_OVER], over_d.rearrange("n o -> o n")[:, 0:MAX_OVER]).then_inc(over_in, 16)
            sp.dma_start(over_row[0:1, 31:32], over_d.rearrange("n o -> o n")[:, 31:32]).then_inc(over_in, 16)
            sp.wait_ge(scattered, 16 * 2 * NT)
            sp.dma_start(lidx[:, :], list_d.rearrange("(e s) o -> s (e o)", e=NE)[0:P, :],
                         allow_slow_non_contiguous=True).then_inc(lidx_in, 16)
            for e in range(NE):
                sp.wait_ge(y_ready, e + 1)
                sp.dma_start(y_d[e * P:(e + 1) * P, :], ysb[:, e % 3, :]).then_inc(y_out[e % 3], 16)
                if e + NSLOT < NE:
                    sp.wait_ge(dn_done, e + 1)
                    load_e(e + NSLOT)
            sp.dma_start(gfin, a["gfin"]).then_inc(gfin_in, 16)
            for t in range(NT):
                sp.wait_ge(fin_ready, t + 1)
                dst = a["o_y"][t * P:(t + 1) * P, :] if t < NPT else a["o_ys"]
                sp.dma_start(dst, x2[:, t, :]).then_inc(fin_out, 16)
            sp.wait_ge(fin_out, 16 * NT)
            for s in range(6):
                sp.wait_ge(nat_out[s], out_count(s, N_K))
            sp.wait_ge(v_out, 160)
            for s in range(2):
                sp.wait_ge(pool_out[s], 128)

        @block.tensor
        def _(pe):
            mm = nc.tensor.matmul
            pe.wait_ge(ones_ready, 1)
            for k in range(KD):
                pe.wait_ge(sq_ready, k + 1)
                for j, (c0, c1) in enumerate(COL3):
                    last = mm(bank[j][:, 0:c1 - c0], ones_f, sq[:, k % 2, c0:c1],
                              start=(k == 0), stop=(k == KD - 1))
                last.then_inc(sq_used, 1)

            def three(out, st_hi, st_lo, mv_hi, mv_lo, ready=None):
                for k in range(KD):
                    if ready is not None:
                        pe.wait_ge(ready, k + 1)
                    mm(out, st_hi(k), mv_hi(k), start=(k == 0), stop=False)
                    mm(out, st_hi(k), mv_lo(k), start=False, stop=False)
                    last = mm(out, st_lo(k), mv_hi(k), start=False, stop=(k == KD - 1))
                return last

            def bank_free(u):
                if u >= 4:
                    pe.wait_ge(pj_evac, u - 3)
                return bank[u % 4]

            def proj_nat(key):
                kind, b, tt = key
                n = first_tile(key)
                if n is not None:
                    pe.wait_ge(w_lo_done, 4 * n + 4)
                s = [i for i, pc in enumerate(PIECES) if pc[0:2] == (kind, b)][0] % 2
                wd = ID + IH if kind == "ki" else 256
                c0 = tcols(tt)[0]
                u = U[key]
                three(bank_free(u)[:, 0:wd], lambda k: h_hi[:, k, c0:c0 + P], lambda k: h_lo[:, k, c0:c0 + P],
                      lambda k: w_hi(s, wd)[:, k, :], lambda k: w_lo(s, wd)[:, k, :],
                      h_ready if u == 0 else None).then_inc(pj_done, 1)

            def trans(key):
                kind, b, tt = key
                if kind == "v":
                    return
                rows = tcols(tt)[1]
                r = RI[key]
                pe.wait_ge(rope_done, r + 1)
                if r >= 2:
                    pe.wait_ge(tr_evac, r - 1)
                bk = bank[4 + r % 2]
                src = nbuf[0:rows, r % 6, :]
                idn = ident[0:rows, 0:rows]
                if kind == "ki":
                    last = nc.tensor.transpose(bk[:, 0:rows], src[:, 0:P], idn)
                elif kind == "qi" and tt == 9:
                    for j in range(4):
                        last = nc.tensor.transpose(bk[:, j * P:(j + 1) * P],
                                                   idxd[:, j, :, :].rearrange("p u d -> p (u d)"), idn)
                else:
                    for j in range(2):
                        last = nc.tensor.transpose(bk[:, j * P:j * P + rows], src[:, j * P:(j + 1) * P], idn)
                last.then_inc(tr_done, 1)

            def nat_run(run):
                for i in range(len(run) + LAG):
                    if i < len(run):
                        proj_nat(run[i])
                    if i >= LAG:
                        trans(run[i - LAG])

            nat_run(RUNS[0])
            pe.wait_ge(tr_evac, N_IDX)
            pe.wait_ge(kic_in, 16)
            for s, (i, (c0, c1), h) in enumerate(SCU):
                if s >= 2:
                    pe.wait_ge(sc_relu, s - 1)
                b = bank[6 + s % 2][:, 0:c1 - c0]
                if i < 8:
                    o = ID * (h % 2)
                    last = mm(b, qiT[o:o + ID, h // 2, i * P:(i + 1) * P], kiT[o:o + ID, c0:c1], start=True, stop=True)
                else:
                    for q in range(4):
                        last = mm(b, qiB[:, h, q * P:(q + 1) * P], kiC[:, q, c0:c1], start=(q == 0), stop=(q == 3))
                last.then_inc(sc_done, 1)
            nat_run(RUNS[1])

            def pool_prod(g):
                pe.wait_ge(win_done, 2 * g + 2)
                pe.wait_ge(wp_in[g % 2], 16 * (g // 2 + 1))
                for cc in range(2):
                    for j, (c0, c1) in enumerate(TOK3):
                        b = bank_free(U["pool", g, (cc, j)])
                        for k in range(2):
                            last = mm(b[:, 0:384], wpool[:, g % 2, k, cc * P:(cc + 1) * P], dT[:, k, c0:c1],
                                      start=(k == 0), stop=(k == 1))
                        last.then_inc(pj_done, 1)

            for n, (kind, b, _, _) in enumerate(PIECES):
                if kind not in ("z", "ga", "gb"):
                    continue
                pe.wait_ge(w_lo_done, 4 * n + 4)
                for cc in range(2):
                    for j, (c0, c1) in enumerate(COL3 if kind == "z" else TOK3):
                        o = 0 if kind == "z" else META
                        three(bank_free(U[kind, b, (cc, j)])[:, 0:c1 - c0],
                              lambda k: w_hi(n % 2)[:, k, cc * P:(cc + 1) * P],
                              lambda k: w_lo(n % 2)[:, k, cc * P:(cc + 1) * P],
                              lambda k: h_hi[:, k, o + c0:o + c1],
                              lambda k: h_lo[:, k, o + c0:o + c1]).then_inc(pj_done, 1)
                if n in AFTER:
                    pool_prod(AFTER[n])
            nat_run(RUNS[2])

            def qk(G, r):
                kind, i, g = AG[G]
                for m, (c0, c1) in enumerate(chunks_of(G)):
                    s = S_AT[G] + r * len(chunks_of(G)) + m
                    if s >= 3:
                        pe.wait_ge(a_sm, s - 2)
                    b = bank[s % 3]
                    if kind == "p":
                        last = mm(b[:, 0:c1 - c0], qT[:, REP * g + r, i * P:(i + 1) * P], kT[:, g, c0:c1],
                                  start=True, stop=True)
                    else:
                        if m == 0:
                            pe.wait_ge(kb_in[i % 3], 64 * (i // 3 + 1))
                            pe.wait_ge(kb_new, i + 1)
                        kt = kTb[:, i % 3, :].rearrange("p (g n) -> p g n", g=KVH)
                        mm(b[:, 0:c1 - c0], repb[:, i, :], sbias[:, c0:c1], start=True, stop=False,
                           skip_group_check=True)
                        for gg in range(KVH):
                            q_b = qsb[:, i % 3, 64 * gg:64 * gg + 64]
                            last = mm(b[64 * gg:64 * gg + 64, 0:c1 - c0], q_b, kt[:, gg, c0:c1],
                                      start=False, stop=True, skip_group_check=True)
                    last.then_inc(a_s, 1)

            def tpv(G):
                kind, i, g = AG[G]
                pe.wait_ge(a_p, U_AT[G + 1])
                ob = bank[5 + G % 2]
                if G >= 2:
                    pe.wait_ge(a_oe, G - 1)
                pb = PB[G % 2]
                if kind == "p":
                    nb = trs_of(G)
                    for j in range(nb + 2):
                        if j < nb:
                            t = T_AT[G] + j
                            if t >= 2:
                                pe.wait_ge(a_te, t - 1)
                            rows = META if j == 0 else P
                            k0 = 0 if j == 0 else META + P * (j - 1)
                            for r in range(REP):
                                last = nc.tensor.transpose(bank[3 + t % 2][0:rows, r * P:(r + 1) * P],
                                                           pb[:, r, k0:k0 + rows], ident)
                            last.then_inc(a_t, 1)
                        if j >= 2:
                            jj = j - 2
                            t = T_AT[G] + jj
                            pe.wait_ge(a_te, t + 1)
                            rows = META if jj == 0 else P
                            last = mm(ob[:, :], vS[0:rows, jj, g * HD:(g + 1) * HD], PT[0:rows, t % 4, :],
                                      start=(jj == 0), stop=(jj == nb - 1))
                    last.then_inc(a_o, 1)
                else:
                    t = T_AT[G]
                    pe.wait_ge(a_te, t - 1)
                    for j in range(4):
                        last = nc.tensor.transpose(bank[3 + t % 2][:, j * P:(j + 1) * P], pb[:, 0, j * P:(j + 1) * P], ident)
                    last.then_inc(a_t, 1)
                    pe.wait_ge(a_te, t)
                    nc.tensor.transpose(bank[3 + (t + 1) % 2][0:32, 0:P], pb[:, 0, 512:SK], ident).then_inc(a_t, 1)
                    pe.wait_ge(a_te, t + 2)
                    v = vb[:, i % 3, :].rearrange("p (j d) -> p j d", j=5)
                    for gg in range(KVH):
                        for j in range(5):
                            rows = P if j < 4 else 32
                            src = PT[0:rows, t % 4, j * P:(j + 1) * P] if j < 4 else PT[0:rows, (t + 1) % 4, 0:P]
                            last = mm(ob[:, 64 * gg:64 * gg + 64], v[0:rows, j, gg * HD:(gg + 1) * HD],
                                      src[:, 64 * gg:64 * gg + 64], start=(j == 0), stop=(j == 4),
                                      skip_group_check=True)
                    last.then_inc(a_o, 1)

            pe.wait_ge(tr_evac, len(ROPED))
            pe.wait_ge(pj_evac, NU)
            for G in range(-1, len(AG)):
                if G + 1 < len(AG):
                    if G + 1 == 2 * NPT:
                        pe.wait_ge(selected, 8)
                    for r in range(heads_of(G + 1)):
                        qk(G + 1, r)
                if G >= 0:
                    tpv(G)

            pe.wait_ge(wao_in, 32)
            pe.wait_ge(a_oe, len(AG))
            for c in range(KD):
                for j, (c0, c1) in enumerate(TOK3):
                    u = 3 * c + j
                    if u >= 4:
                        pe.wait_ge(b6_evac, u - 3)
                    for h in range(HEADS):
                        last = mm(bank[u % 4][:, 0:384], wao[h // 4][:, h % 4, c * P:(c + 1) * P], qT[:, h, c0:c1],
                                  start=(h == 0), stop=(h == HEADS - 1))
                    last.then_inc(b6_done, 1)

            def out_proj(t):
                for hf in range(2):
                    u = 2 * t + hf
                    if u >= 2:
                        pe.wait_ge(x2_ready, u - 1)
                    for k in range(KD):
                        last = mm(bank[4 + hf][:, :], mT[:, k, t * P:(t + 1) * P], wout[:, k, hf * 512:(hf + 1) * 512],
                                  start=(k == 0), stop=(k == KD - 1))
                    last.then_inc(o7_done, 1)

            def router(t):
                pe.wait_ge(h2_ready, t + 1)
                for hf in range(2):
                    u = 2 * t + hf
                    if u >= 2:
                        pe.wait_ge(t7_evac, u - 1)
                    for j in range(4):
                        k = 4 * hf + j
                        last = nc.tensor.transpose(bank[6 + hf][:, j * P:(j + 1) * P], h2[:, t % 2, k * P:(k + 1) * P], ident)
                    last.then_inc(t7_done, 1)
                pe.wait_ge(t7_evac, 2 * t + 2)
                if t >= 2:
                    pe.wait_ge(pos_ready, t - 1)
                for k in range(KD):
                    last = mm(bank[t % 2][:, 0:NG + NE], h2T[:, k, :], wrout[:, k, :], start=(k == 0), stop=(k == KD - 1))
                last.then_inc(lg_done, 1)

            def rank(t):
                pe.wait_ge(hot_ready, t + 1)
                mm(bank[t % 2][:, 64:64 + NE], upper, a_bf[:, t, :], start=True, stop=False, skip_group_check=True)
                mm(bank[t % 2][:, 64:64 + NE], onesb, onehots[:, t, :], start=False, stop=True,
                   skip_group_check=True).then_inc(rank_done, 1)

            pe.wait_ge(m_ready, 24)
            pe.wait_ge(wo_in, 16)
            pe.wait_ge(b6_evac, 24)
            for t in range(NT + 2):
                if t < NT:
                    out_proj(t)
                if 1 <= t <= NT:
                    router(t - 1)
                if t >= 2:
                    rank(t - 2)
            pe.wait_ge(pos_ready, NT)
            mm(bank[2][:, 0:NE], onesb, onehots[:, NT, :], start=True, stop=True).then_inc(cnt_done, 1)

            def e_trans(e):
                pe.wait_ge(hg_in[e % 3], 16 * (e // 3 + 1))
                for hf in range(2):
                    u = 2 * e + hf
                    if u >= 2:
                        pe.wait_ge(te_evac, u - 1)
                    for j in range(4):
                        k = 4 * hf + j
                        last = nc.tensor.transpose(bank[4 + hf][:, j * P:(j + 1) * P], hg[:, e % 3, k * P:(k + 1) * P], ident)
                    last.then_inc(te_done, 1)

            def gate_up(e, slot, par):
                for w, o in ((e_gate(slot), 0), (e_up(slot), P)):
                    for k in range(KD):
                        last = mm(bank[6 + par][:, o:o + P], w[:, k, :], hgT[:, par, k, :],
                                  start=(k == 0), stop=(k == KD - 1), skip_group_check=True)
                last.then_inc(gu_done, 1)

            def down(slot, par):
                for hf in range(2):
                    last = mm(bank[2 * par + hf][:, :], actT[:, par, :], e_down(slot)[:, hf * 512:(hf + 1) * 512],
                              start=True, stop=True)
                last.then_inc(dn_done, 1)

            pe.wait_ge(x2_ready, 2 * NT)
            pe.wait_ge(over_ready, 1)
            e_trans(0)
            for e in range(NE):
                pe.wait_ge(ew_in[e % NSLOT], 48 * (e // NSLOT + 1))
                pe.wait_ge(te_evac, 2 * e + 2)
                if e >= 2:
                    pe.wait_ge(act_ready, e - 1)
                gate_up(e, e % NSLOT, e % 2)
                if e + 1 < NE:
                    e_trans(e + 1)
                pe.wait_ge(act_ready, e + 1)
                if e >= 2:
                    pe.wait_ge(y_ready, e - 1)
                down(e % NSLOT, e % 2)

            pe.wait_ge(over_in, 32)
            n_over = pe.value_load(over_row[0:1, 31:32], min_val=0, max_val=MAX_OVER)
            with pe.If(n_over > 0):
                with pe.Fori(0, n_over) as it:
                    pe.wait_ge(ov_h, 16 * it + 16)
                    for hf in range(2):
                        for j in range(4):
                            k = 4 * hf + j
                            last = nc.tensor.transpose(bank[4 + hf][:, j * P:(j + 1) * P], hg[:, 0, k * P:(k + 1) * P], ident)
                    last.then_inc(te_done, 1)
                    pe.wait_ge(te_evac, 2 * NE + 1 + it)
                    pe.wait_ge(ov_w, 48 * it + 48)
                    gate_up(0, 0, 0)
                    pe.wait_ge(act_ready, NE + 1 + it)
                    down(0, 0)

        @block.scalar
        def _(act):
            cp = nc.scalar.copy
            for k in range(KD):
                act.wait_ge(x_in[k], 16)
                if k >= 2:
                    act.wait_ge(sq_used, k - 1)
                nc.scalar.activation(sq[:, k % 2, :], xk[:, k, :], ACT.Square).then_inc(sq_ready, 1)

            def split_hi(n):
                if n >= 2:
                    act.wait_ge(pj_done, W_LAST[n - 2])
                wd = PIECES[n][3]
                for m in range(4):
                    s = 4 * n + m
                    act.wait_ge(stage_in[s % 4], 16 * (s // 4 + 1))
                    cp(w_hi(n % 2, wd)[:, 2 * m:2 * m + 2, :], stage(s % 4, wd)).then_inc(w_hi_done, 1)

            split_hi(0)
            act.wait_ge(r_ready, 3)
            nc.scalar.activation(rbc, rbc, ACT.Sqrt).then_inc(root_ready, 1)
            for k in range(KD):
                act.wait_ge(h_full, k + 1)
                cp(h_hi[:, k, :], xk[:, k, :]).then_inc(h_high, 1)
            split_hi(1)

            def evac_nat(key):
                kind, b, tt = key
                rows = tcols(tt)[1]
                act.wait_ge(pj_done, U[key] + 1)
                bk = bank[U[key] % 4]
                if kind == "v":
                    cp(vS[0:rows, tt, :], bk[0:rows, 0:256]).then_inc(pj_evac, 1)
                    return
                r = RI[key]
                if r >= 6:
                    act.wait_ge(tr_done, r - 5)
                    if out_count(r % 6, r):
                        act.wait_ge(nat_out[r % 6], out_count(r % 6, r))
                if kind == "ki":
                    cp(nbuf[0:rows, r % 6, 0:ID], bk[0:rows, 0:ID])
                    nc.scalar.mul(wis[0:rows, tt, :], bk[0:rows, ID:ID + IH], IDX_SCALE).then_inc(pj_evac, 1)
                else:
                    cp(nbuf[0:rows, r % 6, :], bk[0:rows, 0:256]).then_inc(pj_evac, 1)

            def evac_tr(key):
                kind, b, tt = key
                if kind == "v":
                    return
                c0, rows = tcols(tt)
                r = RI[key]
                act.wait_ge(tr_done, r + 1)
                bk = bank[4 + r % 2]
                if kind == "ki" and tt < 9:
                    cp(kiT[:, c0:c0 + rows], bk[:, 0:rows]).then_inc(tr_evac, 1)
                elif kind == "ki":
                    act.wait_ge(kic_in, 16)
                    for u in range(2):
                        src = bk[64 * u:64 * u + 64, 0:P].rearrange("p (q x) -> p q x", x=32)
                        last = cp(kiC[64 * u:64 * u + 64, :, CACHE:SK], src[:, :, 16 * u:16 * u + 16])
                    last.then_inc(tr_evac, 1)
                elif kind == "qi" and tt < 9:
                    cp(qiT[:, :, c0 - META:c0 - META + P],
                       bk[:, 0:256].rearrange("p (j t) -> p j t", j=2)).then_inc(tr_evac, 1)
                elif kind == "qi":
                    act.wait_ge(qib_zero, 1)
                    for u in range(2):
                        dst = qiB[64 * u:64 * u + 64, :, :].rearrange("p h (q x) -> p h q x", x=160)
                        src = bk[64 * u:64 * u + 64, :].rearrange("p (h q x) -> p h q x", h=4, x=32)
                        for h in range(IH):
                            last = cp(dst[:, h, :, 16 * u:16 * u + 16], src[:, h, :, 16 * u:16 * u + 16])
                    last.then_inc(tr_evac, 1)
                elif kind == "k":
                    src = bk[:, 0:256].rearrange("p (g t) -> p g t", g=2)
                    cp(kT[:, :, c0:c0 + rows], src[:, :, 0:rows]).then_inc(tr_evac, 1)
                else:
                    cp(qT[:, 2 * b:2 * b + 2, c0 - META:c0 - META + P],
                       bk[:, 0:256].rearrange("p (j t) -> p j t", j=2)).then_inc(tr_evac, 1)

            def nat_run(run):
                for i in range(len(run) + LAG):
                    if i < len(run):
                        n = first_tile(run[i])
                        if n is not None and n >= 1 and n + 1 < NPC:
                            split_hi(n + 1)
                        evac_nat(run[i])
                    if i >= LAG:
                        evac_tr(run[i - LAG])

            act.wait_ge(h_ready, KD)
            act.wait_ge(const_in, 112)
            nat_run(RUNS[0])
            act.wait_ge(list_init, 16)
            for s, (i, (c0, c1), h) in enumerate(SCU):
                act.wait_ge(sc_done, s + 1)
                if s >= 2:
                    act.wait_ge(sc_acc, s - 1)
                nc.scalar.activation(rel[:, s % 2, 0:c1 - c0], bank[6 + s % 2][:, 0:c1 - c0], ACT.Relu).then_inc(sc_relu, 1)
            nat_run(RUNS[1])

            def pool_evac(g):
                for cc in range(2):
                    c = 2 * g + cc
                    act.wait_ge(pool_out[cc], 32 * (g + 1))
                    for j, (c0, c1) in enumerate(TOK3):
                        u = U["pool", g, (cc, j)]
                        act.wait_ge(pj_done, u + 1)
                        nc.scalar.mul(zT[:, cc, c0:c1], bank[u % 4][:, 0:384], pscale[:, c:c + 1]).then_inc(pj_evac, 1)

            for n, (kind, b, _, _) in enumerate(PIECES):
                if kind not in ("z", "ga", "gb"):
                    continue
                split_hi(n + 1)
                for cc in range(2):
                    c = 2 * b + cc
                    if kind == "z":
                        if b >= 1:
                            act.wait_ge(u_out[cc], 16 * b)
                    elif kind == "ga" and b >= 1:
                        act.wait_ge(u_done, c - 1)
                    elif kind == "gb":
                        if b == 0:
                            act.wait_ge(u_done, 7 + cc)
                        else:
                            act.wait_ge(sb_out[cc], 16 * b)
                    for j, (c0, c1) in enumerate(COL3 if kind == "z" else TOK3):
                        u = U[kind, b, (cc, j)]
                        act.wait_ge(pj_done, u + 1)
                        if kind == "z":
                            cp(zT[:, cc, c0:c1], bank[u % 4][:, 0:c1 - c0]).then_inc(pj_evac, 1)
                        else:
                            nc.scalar.activation(sg[:, cc, c0:c1], bank[u % 4][:, 0:384], ACT.Sigmoid).then_inc(pj_evac, 1)
                    if kind == "gb":
                        act.wait_ge(pj_evac, u + 1)
                        act.dma_start(sB_d[c, :, :], sg[:, cc, :]).then_inc(sb_out[cc], 16)
                if n in AFTER:
                    pool_evac(AFTER[n])
            for s in range(2):
                act.wait_ge(u_out[s], 64)
                act.wait_ge(sb_out[s], 64)
                act.wait_ge(pool_out[s], 128)
            nat_run(RUNS[2])

            def expo(G, r):
                uu = U_AT[G] + r
                n = chunks_of(G)[-1][1]
                act.wait_ge(a_max, uu + 1)
                p = PB[G % 2][:, r, 0:n]
                nc.scalar.activation(p, p, ACT.Exp, bias=nmx[:, uu % 8:uu % 8 + 1], scale=ATTN_SCALE,
                                     accum_out=rsum[:, uu % 8:uu % 8 + 1]).then_inc(a_exp, 1)

            def tevac(G, j):
                kind = AG[G][0]
                t = T_AT[G] + j
                act.wait_ge(a_t, t + 1)
                if kind == "p":
                    rows = META if j == 0 else P
                    cp(PT[0:rows, t % 4, :], bank[3 + t % 2][0:rows, :]).then_inc(a_te, 1)
                elif j == 0:
                    cp(PT[:, t % 4, :], bank[3 + t % 2][:, :]).then_inc(a_te, 1)
                else:
                    cp(PT[0:32, t % 4, 0:P], bank[3 + t % 2][0:32, 0:P]).then_inc(a_te, 1)

            for G in range(-1, len(AG)):
                nxt = list(range(heads_of(G + 1))) if G + 1 < len(AG) else []
                cur = list(range(trs_of(G))) if G >= 0 else []
                for r in nxt[:3]:
                    expo(G + 1, r)
                for j in cur[:2]:
                    tevac(G, j)
                for r in nxt[3:]:
                    expo(G + 1, r)
                for j in cur[2:]:
                    tevac(G, j)

            def norm2(t):
                act.wait_ge(x2_ready, 2 * t + 2)
                if t >= 2:
                    act.wait_ge(t7_done, 2 * t - 2)
                    act.wait_ge(h2_out[t % 2], 16 * (t // 2))
                nc.scalar.activation(h2[:, t % 2, :], x2[:, t, :], ACT.Square, scale=1.0 / 32.0,
                                     accum_out=tnrm[:, t, 0:1]).then_inc(ms_ready, 1)

            def h2t(t):
                for hf in range(2):
                    act.wait_ge(t7_done, 2 * t + hf + 1)
                    if t >= 1:
                        act.wait_ge(lg_done, t)
                    cp(h2T[:, 4 * hf:4 * hf + 4, :], bank[6 + hf][:, :].rearrange("p (k t) -> p k t", k=4)).then_inc(t7_evac, 1)

            def route_exp(t):
                act.wait_ge(gexp_in, t + 1)
                nc.scalar.activation(r_gexp, r_lg[:, 0:NG], ACT.Exp, bias=r_ngm, accum_out=r_gs).then_inc(gexp_done, 1)
                act.wait_ge(eexp_in, t + 1)
                nc.scalar.activation(r_ex, r_dv, ACT.Exp).then_inc(eexp_done, 1)

            act.wait_ge(b6_evac, 24)
            act.wait_ge(m_ready, 24)
            for t in range(NT + 1):
                if t < NT:
                    norm2(t)
                if t >= 1:
                    h2t(t - 1)
                    route_exp(t - 1)

            def silu_e(par):
                nc.scalar.activation(silu[:, par, :], bank[6 + par][:, 0:P], ACT.Silu).then_inc(silu_done, 1)

            act.wait_ge(o7_done, 2 * NT)
            for e in range(NE):
                if e < NE:
                    for hf in range(2):
                        act.wait_ge(te_done, 2 * e + hf + 1)
                        if e >= 2:
                            act.wait_ge(gu_done, e - 1)
                        cp(hgT[:, e % 2, 4 * hf:4 * hf + 4, :],
                           bank[4 + hf][:, :].rearrange("p (k t) -> p k t", k=4)).then_inc(te_evac, 1)
                    act.wait_ge(gu_done, e + 1)
                    if e >= 2:
                        act.wait_ge(act_ready, e - 1)
                    silu_e(e % 2)
            act.wait_ge(over_in, 32)
            n_over = act.value_load(over_row[0:1, 31:32], min_val=0, max_val=MAX_OVER)
            with act.If(n_over > 0):
                with act.Fori(0, n_over) as it:
                    act.wait_ge(te_done, 2 * NE + 1 + it)
                    for hf in range(2):
                        last = cp(hgT[:, 0, 4 * hf:4 * hf + 4, :], bank[4 + hf][:, :].rearrange("p (k t) -> p k t", k=4))
                    last.then_inc(te_evac, 1)
                    act.wait_ge(gu_done, NE + 1 + it)
                    silu_e(0)
            for t in range(NT):
                act.wait_ge(y1_done, t + 1)
                nc.scalar.activation(ya[:, t % 2, :], x2[:, t, :], ACT.Square, scale=1.0 / 32.0,
                                     accum_out=fnrm[:, t, 0:1]).then_inc(fms_ready, 1)

        @block.vector
        def _(dve):
            tt = nc.vector.tensor_tensor
            ts = nc.vector.tensor_scalar
            stt = nc.vector.scalar_tensor_tensor
            dve_n = [0]

            def link(ins):
                dve_n[0] += 1
                ins.then_inc(dve_c, 1)
                dve.wait_ge(dve_c, dve_n[0])

            nc.vector.memset(ones_f, 1.0 / D).then_inc(ones_ready, 1)
            dve.wait_ge(const_in, 112)
            dve.wait_ge(sq_used, KD)
            for j, (c0, c1) in enumerate(COL3):
                ts(rbc[:, c0:c1], bank[j][:, 0:c1 - c0], EPS, None, ALU.add).then_inc(r_ready, 1)
            dve.wait_ge(root_ready, 1)
            link(nc.vector.reciprocal(rbc, rbc))
            def h_rest(k):
                dve.wait_ge(h_high, k + 1)
                tt(h_lo[:, k, :], xk[:, k, :], h_hi[:, k, :].bitcast(F32), ALU.subtract).then_inc(h_ready, 1)

            for k in range(KD):
                stt(out=xk[:, k, :], in0=xk[:, k, :], scalar=gmix[:, k:k + 1], in1=rbc,
                    op0=ALU.mult, op1=ALU.mult).then_inc(h_full, 1)
                if k >= 1:
                    h_rest(k - 1)
            h_rest(KD - 1)
            dve.wait_ge(h_ready, KD)
            nc.vector.memset(qiB[:, :, :], 0.0).then_inc(qib_zero, 1)
            link(nc.vector.memset(sc_s[:, SK:SK + 4], 3.0e38))
            for s, (i, (c0, c1), h) in enumerate(SCU):
                dst = (sc[i] if i < 8 else sc_s)[:, c0:c1]
                w = wis[:, i + 1, h:h + 1]
                dve.wait_ge(sc_relu, s + 1)
                if h == 0:
                    ts(dst, rel[:, s % 2, 0:c1 - c0], w, None, ALU.mult).then_inc(sc_acc, 1)
                else:
                    dve.wait_ge(sc_acc, s)
                    stt(out=dst, in0=rel[:, s % 2, 0:c1 - c0], scalar=w, in1=dst,
                        op0=ALU.mult, op1=ALU.add).then_inc(sc_acc, 1)
            dve.wait_ge(sc_acc, len(SCU))
            for i in range(1, NPT):
                link(nc.vector.memset(sc[i][0:64, n_keys[i] - CHUNK:n_keys[i]], MASKED))

            def rounds(tiles, n):
                base = dve_n[0]
                step = 2 * len(tiles)
                with dve.Fori(0, n) as r:
                    for q, x in enumerate(tiles):
                        nc.vector.max(m8[:, q, :], x).then_inc(dve_c, 1)
                    dve.wait_ge(dve_c, step * r + (base + len(tiles)))
                    nc.vector.memset(vjunk, 0.0)
                    for q, x in enumerate(tiles):
                        nc.vector.match_replace(x, m8[:, q, :], x, TAKEN).then_inc(dve_c, 1)
                    dve.wait_ge(dve_c, step * r + (base + step))
                dve_n[0] += step * n

            def bias_of(i):
                if i == 8:
                    ts(sbias[:, :], sc_s[:, 0:SK], BETWEEN, NEG_BIAS, ALU.is_gt, ALU.mult).then_inc(selected, 1)
                    return
                link(ts(sc[i], sc[i], BETWEEN, NEG_BIAS, ALU.is_gt, ALU.mult))
                nc.vector.memset(sc[i][0:64, n_keys[i] - CHUNK:n_keys[i]], NEG_BIAS).then_inc(selected, 1)

            link(nc.vector.memset(sc[0], 0.0))
            nc.vector.memset(sc[0][0:64, n_keys[0] - CHUNK:n_keys[0]], NEG_BIAS).then_inc(selected, 1)
            for i in (1, 3, 5):
                rounds([sc[i], sc[i + 1]], TOPK_P // 8)
                bias_of(i)
                bias_of(i + 1)
            n_s = (TOPK_S + 4) // 8
            rounds([sc_s, sc[7]], n_s)
            rounds([sc[7]], TOPK_P // 8 - n_s)
            bias_of(8)
            bias_of(7)

            def ttr(G, r):
                kind, i, g = AG[G]
                uu = U_AT[G] + r
                ch = chunks_of(G)
                if G >= 2:
                    dve.wait_ge(a_t, T_AT[G - 1])
                for m, (c0, c1) in enumerate(ch):
                    s = S_AT[G] + r * len(ch) + m
                    dve.wait_ge(a_s, s + 1)
                    add = sc[i][:, c0:c1] if kind == "p" else zero[:, 0:c1 - c0]
                    dst = mx3[:, uu % 8, m:m + 1]
                    nc.vector.tensor_tensor_reduce(out=PB[G % 2][:, r, c0:c1], in0=bank[s % 3][:, 0:c1 - c0], in1=add,
                                                   scale=1.0, scalar=MASKED, op0=ALU.add, op1=ALU.max,
                                                   accum_out=dst).then_inc(a_sm, 1)
                dve.wait_ge(a_sm, s + 1)
                if len(ch) > 1:
                    link(nc.vector.tensor_reduce(mx1[:, uu % 8:uu % 8 + 1], mx3[:, uu % 8, 0:len(ch)], AX.X, ALU.max))
                    src = mx1[:, uu % 8:uu % 8 + 1]
                else:
                    src = mx3[:, uu % 8, 0:1]
                ts(nmx[:, uu % 8:uu % 8 + 1], src, -ATTN_SCALE, None, ALU.mult).then_inc(a_max, 1)

            def recip(uu):
                dve.wait_ge(a_exp, uu + 1)
                nc.vector.reciprocal(rinv[:, uu % 8:uu % 8 + 1], rsum[:, uu % 8:uu % 8 + 1]).then_inc(a_ri, 1)

            def oevac(G):
                kind, i, g = AG[G]
                dve.wait_ge(a_o, G + 1)
                ob = bank[5 + G % 2]
                if kind == "p":
                    nc.vector.tensor_copy(qT[:, REP * g:REP * g + REP, i * P:(i + 1) * P],
                                          ob[:, :].rearrange("p (r t) -> p r t", r=REP)).then_inc(a_oe, 1)
                else:
                    nc.vector.tensor_copy(qT[:, :, SEQ + 16 * i:SEQ + 16 * i + 16],
                                          ob[:, 0:P].rearrange("p (r t) -> p r t", r=HEADS)).then_inc(a_oe, 1)

            dve.wait_ge(pj_done, NU)
            nc.vector.memset(zero, 0.0).then_inc(zero_ready, 1)
            dve.wait_ge(zero_ready, 1)
            dve.wait_ge(selected, NT)
            for G in range(-1, len(AG)):
                if G + 1 < len(AG):
                    nh = heads_of(G + 1)
                    for r in range(nh + 1):
                        if r < nh:
                            ttr(G + 1, r)
                        if r >= 1:
                            recip(U_AT[G + 1] + r - 1)
                if G >= 0:
                    oevac(G)

            for c in range(KD):
                dve.wait_ge(sbi_in[c % 2], 16 * (c // 2 + 1))
                dve.wait_ge(mu_in[c // 4], 16)
                for j, (c0, c1) in enumerate(TOK3):
                    u = 3 * c + j
                    dve.wait_ge(b6_done, u + 1)
                    if u >= 2:
                        dve.wait_ge(m_ready, u - 1)
                    tt(mtmp[:, u % 2, :], bank[u % 4][:, 0:384], sB[:, c % 2, c0:c1], ALU.mult).then_inc(b6_evac, 1)
                    dve.wait_ge(b6_evac, u + 1)
                    tt(mT[:, c, c0:c1], mT[:, c, c0:c1], mtmp[:, u % 2, :], ALU.add).then_inc(m_ready, 1)

            def resid(t):
                dve.wait_ge(x2_in, 16)
                for hf in range(2):
                    dve.wait_ge(o7_done, 2 * t + hf + 1)
                    part = x2[:, t, hf * 512:(hf + 1) * 512]
                    tt(part, bank[4 + hf][:, :], part, ALU.add).then_inc(x2_ready, 1)

            def h2_of(t):
                dve.wait_ge(rstd_ready, t + 1)
                stt(out=h2[:, t % 2, :], in0=x2[:, t, :], scalar=tnrm[:, t, 1:2], in1=gffn,
                    op0=ALU.mult, op1=ALU.mult).then_inc(h2_ready, 1)

            def route(t):
                lg = bank[t % 2]
                dve.wait_ge(lg_done, t + 1)
                tt(r_lg[:, 0:NG], lg[:, 0:NG], rbias[:, 0:NG], ALU.add)
                link(tt(r_lg[:, 8:8 + NE], lg[:, NG:NG + NE], rbias[:, NG:NG + NE], ALU.add))
                link(nc.vector.max(r_m8g, r_lg[:, 0:8]))
                ts(r_ngm, r_m8g[:, 0:1], -1.0, None, ALU.mult).then_inc(gexp_in, 1)
                link(nc.vector.max_index(r_i8g, r_m8g, r_lg[:, 0:8]))
                link(nc.vector.tensor_copy(r_gsel, r_i8g[:, 0:1]))
                link(ts(r_mk, iota4, r_gsel, None, ALU.is_equal))
                link(ts(r_mk2, r_mk, 1.0, 3.0e38, ALU.subtract, ALU.mult))
                link(tt(r_em, r_lg[:, 8:8 + NE].rearrange("p (a b) -> p a b", a=NG),
                        r_mk2.unsqueeze(2).to_broadcast([P, NG, EPG]), ALU.add))
                link(nc.vector.max(r_m8e, r_emf))
                link(nc.vector.max_index(r_i8e, r_m8e, r_emf))
                tt(r_dv, r_m8e[:, 1:2], r_m8e[:, 0:1], ALU.subtract).then_inc(eexp_in, 1)
                link(nc.vector.tensor_copy(r_if[:, t, :], r_i8e[:, 0:2]))
                ts(r_oh[:, t, 0:NE], iota32, r_if[:, t, 0:1], None, ALU.is_equal)
                link(ts(r_oh[:, t, NE:2 * NE], iota32, r_if[:, t, 1:2], None, ALU.is_equal))
                link(tt(a_bf[:, t, :], r_oh[:, t, 0:NE], r_oh[:, t, NE:2 * NE], ALU.add))
                tt(onehots[:, t + 1, :], onehots[:, t, :], a_bf[:, t, :], ALU.add).then_inc(hot_ready, 1)
                dve.wait_ge(gexp_done, t + 1)
                dve.wait_ge(eexp_done, t + 1)
                link(ts(r_den, r_ex, 1.0, r_gs, ALU.add, ALU.mult))
                link(nc.vector.reciprocal(wts[:, t, 0:1], r_den))
                link(tt(wts[:, t, 1:2], wts[:, t, 0:1], r_ex, ALU.mult))

            def place(t):
                dve.wait_ge(rank_done, t + 1)
                link(nc.vector.tensor_copy(r_rb, bank[t % 2][:, 64:64 + NE]))
                for q in range(2):
                    link(nc.vector.tensor_tensor_reduce(out=r_junk[:, q, :], in0=r_oh[:, t, q * NE:(q + 1) * NE],
                                                        in1=r_rb, scale=1.0, scalar=0.0, op0=ALU.mult, op1=ALU.add,
                                                        accum_out=r_rank[:, t, q:q + 1]))
                link(stt(out=r_pos, in0=r_if[:, t, :], scalar=float(TOK), in1=r_rank[:, t, :], op0=ALU.mult, op1=ALU.add))
                nc.vector.tensor_copy(posi[:, t, :], r_pos).then_inc(pos_ready, 1)
                dve.wait_ge(pos_ready, t + 1)

            dve.wait_ge(g2_in, 16)
            dve.wait_ge(m_ready, 3 * KD)
            link(nc.vector.memset(r_lg[:, 4:8], MASKED))
            link(nc.vector.memset(onehots[:, 0, :], 0.0))
            for t in range(NT + 2):
                if t < NT:
                    resid(t)
                    h2_of(t)
                if 1 <= t <= NT:
                    route(t - 1)
                if t >= 2:
                    place(t - 2)
            dve.wait_ge(cnt_done, 1)
            for s in range(2):
                dve.wait_ge(h2_out[s], 16 * ((NT - s + 1) // 2))
            link(nc.vector.memset(f_one, 1.0))
            link(nc.vector.tensor_copy(r_rb, bank[2][:, 0:NE]))
            link(tt(f_flag, r_rb.unsqueeze(2).to_broadcast([P, NE, OVER_J]),
                    overthr.unsqueeze(1).to_broadcast([P, NE, OVER_J]), ALU.is_gt))
            link(nc.vector.tensor_tensor_scan(f_cum, f_one, f_flag.rearrange("p a b -> p (a b)"), 0.0, ALU.mult, ALU.add))
            link(ts(f_junk, f_cum, siota, 0.0, ALU.is_le, ALU.add, accum_out=f_id))
            link(nc.vector.tensor_copy(over_i[:, 0:1], f_id))
            nc.vector.tensor_copy(over_i[:, 1:2], f_cum[:, NE * OVER_J - 1:NE * OVER_J]).then_inc(over_ready, 1)

            link(nc.vector.memset(f_ob[:, 0:1], 0.0))
            link(nc.vector.tensor_copy(f_ob[:, 1:NE], f_cum.rearrange("p (e j) -> p e j", e=NE)[:, 0:NE - 1, OVER_J - 1]))
            link(stt(out=f_ob, in0=f_ob, scalar=float(P), in1=base32, op0=ALU.mult, op1=ALU.add))
            for t in range(NT):
                for q in range(2):
                    link(nc.vector.tensor_tensor_reduce(out=r_junk[:, q, :], in0=r_oh[:, t, q * NE:(q + 1) * NE],
                                                        in1=f_ob, scale=1.0, scalar=0.0, op0=ALU.mult, op1=ALU.add,
                                                        accum_out=r_sel[:, t, q:q + 1]))
            link(stt(out=r_y1, in0=r_rank, scalar=float(P), in1=r_sel, op0=ALU.is_ge, op1=ALU.mult))
            link(stt(out=r_y2, in0=r_if, scalar=float(P), in1=r_rank, op0=ALU.mult, op1=ALU.add))
            link(tt(r_y1, r_y1, r_y2, ALU.add))
            nc.vector.tensor_copy(ypos[:, :, :], r_y1).then_inc(ypos_ready, 1)

            def act_of(par):
                tt(actT[:, par, :], silu[:, par, :], bank[6 + par][:, P:2 * P], ALU.mult).then_inc(act_ready, 1)

            for e in range(NE + 1):
                if e >= 1:
                    y = e - 1
                    dve.wait_ge(dn_done, y + 1)
                    if y >= 3:
                        dve.wait_ge(y_out[y % 3], 16 * (y // 3))
                    nc.vector.tensor_copy(ysb[:, y % 3, 0:512], bank[2 * (y % 2)][:, :])
                    nc.vector.tensor_copy(ysb[:, y % 3, 512:1024], bank[2 * (y % 2) + 1][:, :]).then_inc(y_ready, 1)
                if e < NE:
                    dve.wait_ge(silu_done, e + 1)
                    if e >= 2:
                        dve.wait_ge(dn_done, e - 1)
                    act_of(e % 2)
            dve.wait_ge(over_in, 32)
            for s in range(3):
                dve.wait_ge(y_out[s], 16 * ((NE - s + 2) // 3))
            n_over = dve.value_load(over_row[0:1, 31:32], min_val=0, max_val=MAX_OVER)
            with dve.If(n_over > 0):
                with dve.Fori(0, n_over) as it:
                    dve.wait_ge(silu_done, NE + 1 + it)
                    act_of(0)
                    dve.wait_ge(dn_done, NE + 1 + it)
                    nc.vector.tensor_copy(ysb[:, 0, 0:512], bank[0][:, :])
                    nc.vector.tensor_copy(ysb[:, 0, 512:1024], bank[1][:, :]).then_inc(y_ready, 1)

            dve.wait_ge(gfin_in, 16)

            def combine(t):
                dve.wait_ge(ya_in[t % 2], 16 * (t // 2 + 1))
                link(stt(out=x2[:, t, :], in0=ya[:, t % 2, :], scalar=wts[:, t, 0:1], in1=x2[:, t, :],
                         op0=ALU.mult, op1=ALU.add))
                dve.wait_ge(yb_in[t % 2], 16 * (t // 2 + 1))
                stt(out=x2[:, t, :], in0=yb[:, t % 2, :], scalar=wts[:, t, 1:2], in1=x2[:, t, :],
                    op0=ALU.mult, op1=ALU.add).then_inc(y1_done, 1)

            def final(t):
                dve.wait_ge(frstd_ready, t + 1)
                stt(out=x2[:, t, :], in0=x2[:, t, :], scalar=fnrm[:, t, 1:2], in1=gfin,
                    op0=ALU.mult, op1=ALU.mult).then_inc(fin_ready, 1)

            for t in range(NT + 1):
                if t < NT:
                    combine(t)
                if t >= 1:
                    final(t - 1)

        @block.gpsimd
        def _(pool):
            tt = nc.gpsimd.tensor_tensor
            pool_n = [0]

            def link(ins):
                pool_n[0] += 1
                ins.then_inc(pool_c, 1)
                pool.wait_ge(pool_c, pool_n[0])

            link(nc.gpsimd.memset(mhalf, -0.5))
            link(nc.gpsimd.memset(zero_i, 0))
            pool.dma_start(list_d.rearrange("(p n) o -> p (n o)", p=P), zero_i).then_inc(list_init, 16)

            def split_lo(n):
                wd = PIECES[n][3]
                for m in range(4):
                    s = 4 * n + m
                    pool.wait_ge(w_hi_done, s + 1)
                    tt(w_lo(n % 2, wd)[:, 2 * m:2 * m + 2, :], stage(s % 4, wd),
                       w_hi(n % 2, wd)[:, 2 * m:2 * m + 2, :].bitcast(F32), ALU.subtract).then_inc(w_lo_done, 1)

            def rope(key):
                kind, b, ti = key
                if kind == "v":
                    return
                r = RI[key]
                rows = tcols(ti)[1]
                nh, hd, half, o = {"ki": (1, 64, 8, 32), "qi": (4, 64, 8, 32)}.get(kind, (2, 128, 16, 0))
                x = nbuf[0:rows, r % 6, 0:nh * hd].rearrange("p (h d) -> p h d", h=nh)
                x1, x2_ = x[:, :, 0:half], x[:, :, half:2 * half]
                cos = ropec[0:rows, ti, o:o + half].unsqueeze(1).to_broadcast([rows, nh, half])
                sin = ropec[0:rows, ti, o + half:o + 2 * half].unsqueeze(1).to_broadcast([rows, nh, half])
                t4 = [rope_t[0:rows, q, 0:nh * half].rearrange("p (h d) -> p h d", h=nh) for q in range(4)]
                pool.wait_ge(pj_evac, U[key] + 1)
                if r >= 1:
                    pool.wait_ge(rope_done, r)
                tt(t4[0], x1, cos, ALU.mult)
                tt(t4[1], x2_, sin, ALU.mult)
                tt(t4[2], x2_, cos, ALU.mult)
                link(tt(t4[3], x1, sin, ALU.mult))
                tt(x1, t4[0], t4[1], ALU.subtract)
                last = tt(x2_, t4[2], t4[3], ALU.add)
                if kind == "ki":
                    link(last)
                    last = nc.gpsimd.tensor_copy(nbuf[0:rows, r % 6, ID:2 * ID], nbuf[0:rows, r % 6, 0:ID])
                if kind == "qi" and ti == 9:
                    link(last)
                    src = nbuf[:, r % 6, :].rearrange("p (h d) -> p h d", h=IH)
                    for u in range(2):
                        last = nc.gpsimd.tensor_copy(idxd[:, :, u, :], src)
                last.then_inc(rope_done, 1)

            def nat_run(run):
                for key in run:
                    n = first_tile(key)
                    if n is not None and n >= 1 and n + 1 < NPC:
                        split_lo(n + 1)
                    rope(key)

            split_lo(0)
            split_lo(1)
            pool.wait_ge(const_in, 112)
            nat_run(RUNS[0])
            nat_run(RUNS[1])
            pool.wait_ge(tr_done, N_K)
            for s in range(6):
                pool.wait_ge(nat_out[s], out_count(s, N_K))
            pool.wait_ge(sc_acc, len(SCU))

            def state_in(zi):
                pool.dma_start(zs[:, zi % 2, :, 0:15],
                               a["stateT"][:, zi * P:(zi + 1) * P, :].rearrange("b p s -> p b s")).then_inc(st_in[zi % 2], 16)

            for g in range(2):
                pool.dma_start(wpool[:, g, :, :], a["w_pool"][g].rearrange("(k p) d -> p k d", p=P)).then_inc(wp_in[g], 16)
                state_in(g)

            def windows(g, cc):
                zi = 2 * g + cc
                pool.wait_ge(pj_evac, U["z", g, (cc, 2)] + 1)
                pool.wait_ge(st_in[cc], 16 * (g + 1))
                if cc == 0 and g >= 1:
                    pool.wait_ge(pj_done, U["pool", g - 1, (1, 2)] + 1)
                z, z_s = zT[:, cc, :], zs[:, cc, :, :]
                link(nc.gpsimd.tensor_copy(z_s[:, :, 15:31], z[:, SAMPLE0:COLS].rearrange("p (b s) -> p b s", b=DEC_B)))
                cur, cur_s = z, z_s
                for lv in range(g + 1):
                    sh = 1 << lv
                    lo = 2 * sh - 1
                    nxt, nxt_s = (wa, za) if (g - lv) % 2 == 0 else (dT[:, cc, :], zb)
                    tt(nxt[:, lo:SAMPLE0], cur[:, lo:SAMPLE0], cur[:, lo - sh:SAMPLE0 - sh], ALU.add)
                    link(tt(nxt_s[:, :, lo:31], cur_s[:, :, lo:31], cur_s[:, :, lo - sh:31 - sh], ALU.add))
                    cur, cur_s = nxt, nxt_s
                inv = 1.0 / (2 << g)
                dst_s = dT[:, cc, SEQ:TOK].rearrange("p (b s) -> p b s", b=DEC_B)
                nc.gpsimd.tensor_scalar(cur[:, META:SAMPLE0], cur[:, META:SAMPLE0], inv, None, ALU.mult)
                link(nc.gpsimd.tensor_scalar(cur_s[:, :, 15:31], cur_s[:, :, 15:31], inv, None, ALU.mult))
                tt(dT[:, cc, 0:SEQ], cur[:, META:SAMPLE0], z[:, META:SAMPLE0], ALU.subtract)
                tt(dst_s, cur_s[:, :, 15:31], z_s[:, :, 15:31], ALU.subtract).then_inc(win_done, 1)
                pool.wait_ge(win_done, zi + 1)
                pool.dma_start(a["o_poolT"][zi * P:(zi + 1) * P, :],
                               z[:, SAMPLE0 - POOL_STATE:SAMPLE0]).then_inc(pool_out[cc], 16)
                pool.dma_start(a["o_poolsT"][:, zi * P:(zi + 1) * P, :].rearrange("b p s -> p b s"),
                               z_s[:, :, 16:31]).then_inc(pool_out[cc], 16)

            def gate_mult(g):
                for cc in range(2):
                    c = 2 * g + cc
                    pool.wait_ge(pj_evac, U["pool", g, (cc, 2)] + 1)
                    u = zT[:, cc, 0:TOK]
                    tt(u, u, sg[:, cc, :], ALU.mult).then_inc(u_done, 1)
                    pool.wait_ge(u_done, c + 1)
                    pool.dma_start(uA_d[c, :, :], u).then_inc(u_out[cc], 16)
                if g < 2:
                    pool.dma_start(wpool[:, g, :, :], a["w_pool"][g + 2].rearrange("(k p) d -> p k d", p=P)).then_inc(wp_in[g], 16)

            for n, (kind, b, _, _) in enumerate(PIECES):
                if kind not in ("z", "ga", "gb"):
                    continue
                if kind != "ga":
                    split_lo(n + 1)
                if n in AFTER:
                    gate_mult(AFTER[n])
                if kind == "z":
                    windows(b, 0)
                    split_lo(n + 2)
                    windows(b, 1)
                    if b < 3:
                        for cc in range(2):
                            pool.wait_ge(pool_out[cc], 32 * (b + 1))
                            state_in(2 * b + 2 + cc)
            nat_run(RUNS[2])

            def new_keys(b):
                kt = kTb[:, b % 3, :].rearrange("p (g n) -> p g n", g=KVH)
                if b >= 3:
                    pool.wait_ge(a_o, 2 * NPT + b - 2)
                else:
                    pool.wait_ge(pj_done, NU)
                    pool.wait_ge(tr_evac, len(ROPED))
                nc.gpsimd.tensor_copy(qsb[:, b % 3, :].rearrange("p (h t) -> p h t", h=HEADS),
                                      qT[:, :, SEQ + 16 * b:SEQ + 16 * b + 16])
                nc.gpsimd.tensor_copy(kt[:, :, CACHE:SK],
                                      kT[:, :, SAMPLE0 + 16 * b:SAMPLE0 + 16 * b + 16]).then_inc(kb_new, 1)

            for b in range(3):
                new_keys(b)
            for G in range(len(AG)):
                for r in range(heads_of(G)):
                    uu = U_AT[G] + r
                    p = PB[G % 2][:, r, 0:chunks_of(G)[-1][1]]
                    pool.wait_ge(a_ri, uu + 1)
                    nc.gpsimd.tensor_scalar(p, p, rinv[:, uu % 8:uu % 8 + 1], None, ALU.mult).then_inc(a_p, 1)
                b = G - 2 * NPT + 2
                if 3 <= b < DEC_B:
                    new_keys(b)

            def rstd(nrm, t):
                link(nc.gpsimd.tensor_scalar(nrm[:, t, 1:2], nrm[:, t, 0:1], EPS, None, ALU.add))
                return tt(nrm[:, t, 1:2], nrm[:, t, 1:2], mhalf, ALU.pow)

            for t in range(NT + 2):
                if t < NT:
                    pool.wait_ge(ms_ready, t + 1)
                    rstd(tnrm, t).then_inc(rstd_ready, 1)
                if t < 2:
                    continue
                t -= 2
                if t == 0:
                    pool.wait_ge(list_init, 16)
                pool.wait_ge(pos_ready, t + 1)
                for q in range(2):
                    pool.indirect_dma_start(out=list_d, out_offset=bass.IndirectOffsetOnAxis(ap=posi[:, t, q:q + 1], axis=0),
                                            in_=tokid[:, t:t + 1], in_offset=None).then_inc(scattered, 16)

            def gather(dst, src, idx, s):
                pool.indirect_dma_start(out=dst, out_offset=None, in_=src,
                                        in_offset=bass.IndirectOffsetOnAxis(ap=idx, axis=0)).then_inc(s, 16)

            pool.wait_ge(lidx_in, 16)
            pool.wait_ge(o7_done, 2 * NT)
            for s in range(2):
                pool.wait_ge(h2_out[s], 16 * ((NT - s + 1) // 2))
            for e in range(NE):
                if e >= 3:
                    pool.wait_ge(te_done, 2 * (e - 2))
                gather(hg[:, e % 3, :], h2_d, lidx[:, e:e + 1], hg_in[e % 3])
            pool.wait_ge(over_in, 32)
            n_over = pool.value_load(over_row[0:1, 31:32], min_val=0, max_val=MAX_OVER)
            with pool.If(n_over > 0):
                pool.wait_ge(dn_done, NE)
                with pool.Fori(0, n_over) as it:
                    code = pool.value_load(over_row[0:1, bass.ds(it, 1)], min_val=0, max_val=NE * OVER_J - 1)
                    ex = pool.snap(code // OVER_J, min_val=0, max_val=NE - 1)
                    row = pool.snap((code // OVER_J) * (TOK - P * OVER_J) + code * P + P, min_val=0, max_val=NE * TOK - P)
                    for dst, src in ((e_gate(0), a["wg"]), (e_up(0), a["wu"])):
                        pool.dma_start(dst, src[bass.ds(ex, 1), :, :].rearrange("o (k p) f -> p (o k) f", p=P)).then_inc(ov_w, 16)
                    pool.dma_start(e_down(0), a["wd"][bass.ds(ex, 1), :, :].rearrange("o p f -> p (o f)")).then_inc(ov_w, 16)
                    pool.dma_start(lidx_o[:, :], list_d[bass.ds(row, P), :]).then_inc(ov_l, 16)
                    pool.wait_ge(ov_l, 16 * it + 16)
                    tt(pjunk, mhalf, mhalf, ALU.add).then_inc(ov_c, 1)
                    gather(hg[:, 0, :], h2_d, lidx_o[:, 0:1], ov_h)
                    pool.wait_ge(y_ready, NE + 1 + it)
                    pool.dma_start(y_d[bass.ds(pool.snap(it * P + NE * P, min_val=NE * P, max_val=(NE + MAX_OVER - 1) * P), P), :], ysb[:, 0, :]).then_inc(ov_y, 16)
                    pool.wait_ge(ov_y, 16 * it + 16)
                    pool.wait_ge(ov_c, it + 1)
            for s in range(3):
                pool.wait_ge(y_out[s], 16 * ((NE - s + 2) // 3))
            pool.wait_ge(ypos_ready, 1)
            for t in range(NT + 2):
                if t >= 2:
                    pool.wait_ge(fms_ready, t - 1)
                    rstd(fnrm, t - 2).then_inc(frstd_ready, 1)
                if t < NT:
                    gather(ya[:, t % 2, :], y_d, ypos[:, t, 0:1], ya_in[t % 2])
                    gather(yb[:, t % 2, :], y_d, ypos[:, t, 1:2], yb_in[t % 2])


def _constants():
    pos = [np.arange(META)] + [META + P * i + np.arange(P) for i in range(NPT)]
    pos += [CACHE + np.tile(np.arange(DEC_S), DEC_B)]
    c = np.zeros((P, K_END), np.float32)
    c[:, K_ID:K_ID + P] = np.eye(P)
    for t, p in enumerate(pos):
        col = 0
        for rot in (HD // 4, ID // 4):
            half = rot // 2
            inv = np.exp(np.float32(-math.log(500000.0)) * np.arange(half, dtype=np.float32) * np.float32(2.0 / rot))
            ang = p.astype(np.float32)[:, None] * inv.astype(np.float32)[None, :]
            at = K_ROPE + 48 * t + col
            c[:len(p), at:at + half] = np.cos(ang)
            c[:len(p), at + half:at + 2 * half] = np.sin(ang)
            col += 2 * half
    c[:, K_I32:K_I32 + NE] = np.arange(NE)
    c[:, K_BASE:K_BASE + NE] = P * (NE - 1 - np.arange(NE))
    c[:, K_I4:K_I4 + NG] = np.arange(NG)
    c[:, K_SI] = np.arange(P)
    c[:, K_THR:K_THR + OVER_J] = P * (1 + np.arange(OVER_J))
    one = 0x3F80
    b = np.zeros((P, 10 * P), np.uint16)
    for s in range(DEC_B):
        for m in range(P):
            b[16 * s + m % 16, s * P + m] = one
    b[:, 8 * P:9 * P] = np.triu(np.full((P, P), one, np.uint16), 1)
    b[:, 9 * P:] = one
    tok = (np.arange(NT)[None, :] * P + np.arange(P)[:, None]).astype(np.int32)
    return c, b, tok


def kernel(**inp):
    import concourse.bacc as bacc
    from concourse.bass_utils import run_bass_kernel_spmd

    f = {k: np.asarray(v) for k, v in inp.items()}
    c, b, tok = _constants()
    xp, xs = f["x_prompt"][0], f["x_sample"].reshape(DEC_B * DEC_S, D)
    arrays = {
        "xT": np.concatenate([f["meta_tokens"], xp, xs], axis=0).T,
        "x": np.concatenate([xp, xs], axis=0),
        "gmix": f["norm_mix_g"][0].reshape(KD, P).T,
        "pscale": f["pool_scale"][0].reshape(KD, P).T,
        "gffn": np.broadcast_to(f["norm_ffn_g"][0], (P, D)),
        "gfin": np.broadcast_to(f["norm_final_g"], (P, D)),
        "w_in": f["w_in"][0],
        "w_pool": f["w_pool"][0],
        "w_attn_out": f["w_attn_out"][0],
        "w_out": f["w_out"][0],
        "wrout": np.concatenate([f["w_router_group"][0], f["w_router_expert"][0]], axis=1),
        "rbias": np.broadcast_to(np.concatenate([f["b_router_group"][0], f["b_router_expert"][0]]), (P, NG + NE)),
        "wg": f["w_expert_gate"][0], "wu": f["w_expert_up"][0], "wd": f["w_expert_down"][0],
        "ckT": f["cache_k"][0].transpose(0, 2, 3, 1),
        "cv": f["cache_v"][0].reshape(DEC_B, CACHE, KVH * HD),
        "kiC": f["cache_idx_k"][0].transpose(0, 2, 1).reshape(DEC_B // 2, 2 * ID, CACHE),
        "stateT": f["state_pool"][0].transpose(0, 2, 1),
        "consts": c, "cbf": b, "tokid": tok,
    }
    outs = {"o_y": (SEQ, D), "o_ys": (DEC_B * DEC_S, D), "o_k": (META + SEQ, 256), "o_v": (META + SEQ, 256),
            "o_ki": (META + SEQ, ID), "o_poolT": (D, POOL_STATE), "o_ks": (P, 256), "o_vs": (P, 256), "o_kis": (P, ID),
            "o_poolsT": (DEC_B, D, POOL_STATE)}
    nc = bacc.Bacc("TRN2", target_bir_lowering=False, num_devices=1)
    a, feed = {}, {}
    for name, arr in arrays.items():
        arr = np.ascontiguousarray(arr)
        feed[f"in_{name}"] = arr
        a[name] = nc.dram_tensor(f"in_{name}", arr.shape, mybir.dt.from_np(arr.dtype), kind="ExternalInput").ap()
    for name, shape in outs.items():
        a[name] = nc.dram_tensor(f"out_{name}", shape, F32, kind="ExternalOutput").ap()
    build(nc, a)
    r = run_bass_kernel_spmd(nc, [feed], core_ids=[0]).results[0]
    o = {name: r[f"out_{name}"] for name in outs}
    return (o["o_y"].reshape(1, SEQ, D), o["o_ys"].reshape(DEC_B, DEC_S, D),
            o["o_k"].reshape(1, 1, META + SEQ, KVH, HD), o["o_v"].reshape(1, 1, META + SEQ, KVH, HD),
            o["o_ki"].reshape(1, 1, META + SEQ, ID), o["o_poolT"].T.reshape(1, 1, POOL_STATE, D),
            o["o_ks"].reshape(1, DEC_B, DEC_S, KVH, HD), o["o_vs"].reshape(1, DEC_B, DEC_S, KVH, HD),
            o["o_kis"].reshape(1, DEC_B, DEC_S, ID), o["o_poolsT"].transpose(0, 2, 1).reshape(1, DEC_B, POOL_STATE, D))
```
